# Optimizing a Trainium2 kernel written in Bass

```python
import jax, jax.numpy as jnp
from jax import lax
import numpy as np

D_MODEL = 1024
BATCH = 1
SEQ = 1024
DEPTH = 1
DEC_BATCH = 8
DEC_SEQ = 4
PAST_LEN = 8192
PAGE_SIZE = 128

MIX_WIDTH = D_MODEL
POOL_WIDTH = MIX_WIDTH // 2
CONV_WIDTH = MIX_WIDTH - POOL_WIDTH
POOL_WINDOWS = (2, 4, 8, 16)
N_POOL_GROUPS = len(POOL_WINDOWS)
POOL_GROUP = POOL_WIDTH // N_POOL_GROUPS
POOL_STATE = max(POOL_WINDOWS) - 1
CONV_KERNEL = 31
CONV_STATE = CONV_KERNEL - 1
N_IN = POOL_WIDTH + 2 * CONV_WIDTH
PEER_HEADS = 8
PEER_KEY_DIM = 256
PEER_HALF = PEER_KEY_DIM // 2
N_KEYS = 128
N_EXPERTS = N_KEYS * N_KEYS
PEER_TOPK = 16
PEER_BLOCK = 128
N_MOD = 6
EPS = 1e-6

kernel_name = 'hybrid_pool_conformer_peer_adaln_step'

def rmsnorm(x, g):
    xf = x.astype(jnp.float32)
    y = xf * lax.rsqrt(jnp.mean(xf * xf, axis=-1, keepdims=True) + EPS)
    return (y * g.astype(jnp.float32)).astype(x.dtype)

def layernorm(x, g, b):
    xf = x.astype(jnp.float32)
    mu = jnp.mean(xf, axis=-1, keepdims=True)
    var = jnp.mean(jnp.square(xf - mu), axis=-1, keepdims=True)
    y = (xf - mu) * lax.rsqrt(var + EPS)
    return (y * g.astype(jnp.float32) + b.astype(jnp.float32)).astype(x.dtype)

def token_mixer(h, pool_prefix, conv_prefix, start, w_in, b_in, w_pool, pool_scale,
                conv_w, conv_b, ln_g, ln_b, w_out, b_out):
    B, T, _ = h.shape
    proj = h @ w_in + b_in
    hp = proj[..., :POOL_WIDTH]
    cv = proj[..., POOL_WIDTH:POOL_WIDTH + CONV_WIDTH]
    cg = proj[..., POOL_WIDTH + CONV_WIDTH:]

    zp = jnp.concatenate([pool_prefix.astype(hp.dtype), hp], axis=1)
    cs = jnp.pad(jnp.cumsum(zp.astype(jnp.float32), axis=1), ((0, 0), (1, 0), (0, 0)))
    pos = start + jnp.arange(T, dtype=jnp.int32)
    P = POOL_STATE
    diffs = []
    for gi, w in enumerate(POOL_WINDOWS):
        sl = slice(gi * POOL_GROUP, (gi + 1) * POOL_GROUP)
        wsum = cs[:, P + 1:P + T + 1, sl] - cs[:, P + 1 - w:P + T + 1 - w, sl]
        cnt = jnp.minimum(pos + 1, w).astype(jnp.float32)[None, :, None]
        diffs.append(wsum / cnt - hp[..., sl].astype(jnp.float32))
    d = jnp.stack(diffs, axis=2).astype(hp.dtype)
    pool_out = jnp.einsum('btgc,gcd->btgd', d, w_pool).reshape(B, T, POOL_WIDTH) * pool_scale

    glu = cv * jax.nn.sigmoid(cg)
    zc = jnp.concatenate([conv_prefix.astype(glu.dtype), glu], axis=1)
    conv = lax.conv_general_dilated(zc, conv_w.astype(zc.dtype), (1,), 'VALID',
                                    dimension_numbers=('NWC', 'WIO', 'NWC'),
                                    feature_group_count=CONV_WIDTH) + conv_b
    conv_out = jax.nn.silu(layernorm(conv, ln_g, ln_b))

    mixed = jnp.concatenate([pool_out, conv_out], axis=-1) @ w_out + b_out
    return mixed, zp[:, -POOL_STATE:], zc[:, -CONV_STATE:]

def peer_ffn(h, w_query, sub_keys, u_table, v_table):
    B, T, D = h.shape
    n = B * T
    pad = (-n) % PEER_BLOCK
    hf = jnp.pad(h.reshape(n, D), ((0, pad), (0, 0)))
    q = (hf @ w_query).reshape(-1, PEER_HEADS, 2, PEER_HALF)
    s = jnp.einsum('nhpk,hpmk->nhpm', q.astype(jnp.float32), sub_keys.astype(jnp.float32))
    sv, si = lax.top_k(s, PEER_TOPK)
    comb = (sv[:, :, 0, :, None] + sv[:, :, 1, None, :]).reshape(-1, PEER_HEADS, PEER_TOPK * PEER_TOPK)
    cidx = (si[:, :, 0, :, None] * N_KEYS + si[:, :, 1, None, :]).reshape(-1, PEER_HEADS, PEER_TOPK * PEER_TOPK)
    fv, fpos = lax.top_k(comb, PEER_TOPK)
    eid = jnp.take_along_axis(cidx, fpos, axis=-1)
    gate = jax.nn.softmax(fv, axis=-1).astype(h.dtype)

    nb = hf.shape[0] // PEER_BLOCK
    hb = hf.reshape(nb, PEER_BLOCK, D)
    eb = eid.reshape(nb, PEER_BLOCK, PEER_HEADS, PEER_TOPK)
    gb = gate.reshape(nb, PEER_BLOCK, PEER_HEADS, PEER_TOPK)

    def block(args):
        hx, ex, gx = args
        a = jnp.einsum('phkd,pd->phk', u_table[ex], hx)
        act = jax.nn.gelu(a, approximate=False) * gx
        return jnp.einsum('phk,phkd->pd', act, v_table[ex])

    out = lax.map(block, (hb, eb, gb)).reshape(-1, D)[:n]
    return out.reshape(B, T, D)

def decoder_layer(x, c, pool_prefix, conv_prefix, start, w_ada, b_ada, g_norm1, g_norm2,
                  w_in, b_in, w_pool, pool_scale, conv_w, conv_b, ln_g, ln_b, w_out, b_out,
                  w_query, sub_keys, u_table, v_table):
    mod = jax.nn.silu(c) @ w_ada + b_ada
    sh1, sc1, gt1, sh2, sc2, gt2 = [m[:, None, :] for m in jnp.split(mod, N_MOD, axis=-1)]
    h1 = rmsnorm(x, g_norm1) * (1 + sc1) + sh1
    mix, new_pool, new_conv = token_mixer(h1, pool_prefix, conv_prefix, start, w_in, b_in,
                                          w_pool, pool_scale, conv_w, conv_b, ln_g, ln_b,
                                          w_out, b_out)
    x = x + gt1 * mix
    h2 = rmsnorm(x, g_norm2) * (1 + sc2) + sh2
    x = x + gt2 * peer_ffn(h2, w_query, sub_keys, u_table, v_table)
    return x, new_pool, new_conv

def setup_inputs(seed: int = 0) -> dict:
    key = jax.random.key(seed)
    ks = jax.random.split(key, 24)
    f32 = jnp.float32
    nrm = lambda k, shp, s: (jax.random.normal(k, shp, f32) * s).astype(f32)
    D = D_MODEL
    return {
        'x_prompt': nrm(ks[0], (BATCH, SEQ, D), 1.0),
        'x_sample': nrm(ks[1], (DEC_BATCH, DEC_SEQ, D), 1.0),
        'state_pool': nrm(ks[2], (DEPTH, DEC_BATCH, POOL_STATE, POOL_WIDTH), 1.0),
        'state_conv': nrm(ks[3], (DEPTH, DEC_BATCH, CONV_STATE, CONV_WIDTH), 0.5),
        'c_prompt': nrm(ks[4], (BATCH, D), 1.0),
        'c_sample': nrm(ks[5], (DEC_BATCH, D), 1.0),
        'w_ada': nrm(ks[6], (DEPTH, D, N_MOD * D), 0.5 * D ** -0.5),
        'b_ada': nrm(ks[7], (DEPTH, N_MOD * D), 0.02),
        'g_norm1': 1.0 + nrm(ks[8], (DEPTH, D), 0.05),
        'g_norm2': 1.0 + nrm(ks[9], (DEPTH, D), 0.05),
        'w_in': nrm(ks[10], (DEPTH, D, N_IN), D ** -0.5),
        'b_in': nrm(ks[11], (DEPTH, N_IN), 0.02),
        'w_pool': nrm(ks[12], (DEPTH, N_POOL_GROUPS, POOL_GROUP, POOL_GROUP), POOL_GROUP ** -0.5),
        'pool_scale': 1.0 + nrm(ks[13], (DEPTH, POOL_WIDTH), 0.1),
        'conv_w': nrm(ks[14], (DEPTH, CONV_KERNEL, 1, CONV_WIDTH), CONV_KERNEL ** -0.5),
        'conv_b': nrm(ks[15], (DEPTH, CONV_WIDTH), 0.02),
        'ln_g': 1.0 + nrm(ks[16], (DEPTH, CONV_WIDTH), 0.05),
        'ln_b': nrm(ks[17], (DEPTH, CONV_WIDTH), 0.02),
        'w_out': nrm(ks[18], (DEPTH, MIX_WIDTH, D), MIX_WIDTH ** -0.5),
        'b_out': nrm(ks[19], (DEPTH, D), 0.02),
        'w_query': nrm(ks[20], (DEPTH, D, PEER_HEADS * PEER_KEY_DIM), D ** -0.5),
        'sub_keys': nrm(ks[21], (DEPTH, PEER_HEADS, 2, N_KEYS, PEER_HALF), PEER_HALF ** -0.5),
        'u_table': nrm(ks[22], (DEPTH, N_EXPERTS, D), D ** -0.5),
        'v_table': nrm(ks[23], (DEPTH, N_EXPERTS, D), PEER_HEADS ** -0.5),
        'g_final': 1.0 + nrm(jax.random.fold_in(key, 99), (D,), 0.05),
    }

def reference(x_prompt, x_sample, state_pool, state_conv, c_prompt, c_sample, w_ada, b_ada,
              g_norm1, g_norm2, w_in, b_in, w_pool, pool_scale, conv_w, conv_b, ln_g, ln_b,
              w_out, b_out, w_query, sub_keys, u_table, v_table, g_final):
    xp, xs = x_prompt, x_sample
    pool_p, conv_p, pool_s, conv_s = [], [], [], []
    for l in range(DEPTH):
        zero_pool = jnp.zeros((xp.shape[0], POOL_STATE, POOL_WIDTH), xp.dtype)
        zero_conv = jnp.zeros((xp.shape[0], CONV_STATE, CONV_WIDTH), xp.dtype)
        xp, npp, ncp = decoder_layer(xp, c_prompt, zero_pool, zero_conv, 0,
                                     w_ada[l], b_ada[l], g_norm1[l], g_norm2[l], w_in[l], b_in[l],
                                     w_pool[l], pool_scale[l], conv_w[l], conv_b[l], ln_g[l], ln_b[l],
                                     w_out[l], b_out[l], w_query[l], sub_keys[l], u_table[l], v_table[l])
        xs, nps, ncs = decoder_layer(xs, c_sample, state_pool[l], state_conv[l], PAST_LEN,
                                     w_ada[l], b_ada[l], g_norm1[l], g_norm2[l], w_in[l], b_in[l],
                                     w_pool[l], pool_scale[l], conv_w[l], conv_b[l], ln_g[l], ln_b[l],
                                     w_out[l], b_out[l], w_query[l], sub_keys[l], u_table[l], v_table[l])
        pool_p.append(npp); conv_p.append(ncp); pool_s.append(nps); conv_s.append(ncs)
    y_prompt = rmsnorm(xp, g_final)
    y_sample = rmsnorm(xs, g_final)
    return (y_prompt, y_sample, jnp.stack(pool_p), jnp.stack(conv_p), jnp.stack(pool_s), jnp.stack(conv_s))


_drawn_inputs = setup_inputs


def setup_inputs(seed=0):
    import zlib

    import numpy as np

    out = dict(_drawn_inputs(seed))
    spreads = {}
    factors = {'g_norm2': 4.178,
     'b_in': 2.816,
     'pool_scale': 2.735,
     'conv_b': 8.0,
     'ln_g': 6.482,
     'ln_b': 21.447,
     'b_out': 6.887}
    for name, (base, spread) in spreads.items():
        noise = np.random.default_rng([zlib.crc32(name.encode()), seed]).standard_normal(out[name].shape)
        drawn = base * np.exp(spread * noise) if base else spread * noise
        out[name] = __import__('jax').numpy.asarray(drawn.astype(out[name].dtype))
    for name, factor in factors.items():
        out[name] = (out[name] * factor).astype(out[name].dtype)
    return out
```

```python
from contextlib import ExitStack

import concourse.bass as bass
from concourse import mybir

F32 = mybir.dt.float32
BF16 = mybir.dt.bfloat16
U32 = mybir.dt.uint32
ALU = mybir.AluOpType
ACT = mybir.ActivationFunctionType
AX = mybir.AxisListType.X

P = 128
D = 1024
KC = D // P
T = 1024
NB = T // P
NS = 8
TS = 4
S = NS * TS
NT = T + S
NR = 1 + NS
NMOD = 6
G = 4
WIN = [2, 4, 8, 16]
PS = 15
CK = 31
CS = CK - 1
GW = G * P
EPS = 1e-6
H = 8
K = 16
NKEY = 128
HALF = 512
CH = 4
RING = 2 * CH
CPH = K // CH
SH1, SC1, GT1, SH2, SC2, GT2 = range(NMOD)
REG = [(0, HALF), (HALF, HALF), (T, S)]
FE_PARTS = 4


def build(nc, x_prompt, x_sample, state_pool, state_conv, c_prompt, c_sample, w_ada, b_ada, g_norm1, g_norm2,
          w_in, b_in, w_pool, pool_scale, conv_w, conv_b, ln_g, ln_b, w_out, b_out, w_query, sub_keys,
          u_table, v_table, g_final, y_prompt, y_sample, pool_prompt, conv_prompt, pool_sample, conv_sample):
    x1_dram = nc.dram_tensor("x1_scratch", [NT, D], F32, kind="Internal").ap()
    mod_dram = nc.dram_tensor("mod_scratch", [NR, NMOD * D], F32, kind="Internal").ap()
    with ExitStack() as ctx:
        ps = [ctx.enter_context(nc.psum_tensor(f"bank{i}", [P, HALF], F32)) for i in range(8)]
        ident = ctx.enter_context(nc.sbuf_tensor("ident", [P, P], F32))
        eps_c = ctx.enter_context(nc.sbuf_tensor("eps_c", [P, 1], F32))
        mixer_phase(nc, ps, ident, eps_c, x1_dram, mod_dram, x_prompt, x_sample, state_pool, state_conv, c_prompt,
                    c_sample, w_ada, b_ada, g_norm1, g_norm2, w_in, b_in, w_pool, pool_scale, conv_w, conv_b,
                    ln_g, ln_b, w_out, b_out, pool_prompt, conv_prompt, pool_sample, conv_sample)
        expert_phase(nc, ps, ident, eps_c, x1_dram, mod_dram, w_query, sub_keys, u_table, v_table, g_final,
                     y_prompt, y_sample)


def mixer_phase(nc, ps, ident, eps_c, x1_dram, mod_dram, x_prompt, x_sample, state_pool, state_conv, c_prompt,
                c_sample, w_ada, b_ada, g_norm1, g_norm2, w_in, b_in, w_pool, pool_scale, conv_w, conv_b,
                ln_g, ln_b, w_out, b_out, pool_prompt, conv_prompt, pool_sample, conv_sample):
    with ExitStack() as ctx:
        def sb(name, shape, dt=F32):
            return ctx.enter_context(nc.sbuf_tensor(name, shape, dt))

        def sem(name):
            return ctx.enter_context(nc.semaphore(name))

        wbuf = sb("wbuf", [P, 3 * KC * HALF])
        ada = wbuf[:, :].rearrange("p (r k n) -> p r k n", r=3, k=KC)
        win = wbuf[:, :].rearrange("p (k n) -> p k n", k=KC)
        wout = wbuf[:, 0:KC * D].rearrange("p (k n) -> p k n", k=KC)
        bout = wbuf[0:1, KC * D:KC * D + D]
        rstd_ln = wbuf[:, KC * D + D:KC * D + D + NT]
        ada_b = sb("ada_b", [1, 3, HALF])
        h1t = sb("h1t", [P, KC, NT])
        flat = h1t[:, :, :].rearrange("p k t -> p (k t)")
        csil = flat[0:NR, 0:D]
        sq = flat[:, 0:G * NT].rearrange("p (c t) -> p c t", c=G)
        st_out = flat[0:S, G * NT:G * NT + 4 * GW].rearrange("p (s n) -> p s n", s=4)
        mixt = sb("mixt", [P, 2 * G, NT])
        mflat = mixt[:, :, :].rearrange("p k t -> p (k t)")
        modrow = mflat[0:NR, 0:NMOD * D]
        g1row = mflat[0:NR, NMOD * D:(NMOD + 1) * D]
        g2row = mflat[0:NR, (NMOD + 1) * D:(NMOD + 2) * D]
        xr = sb("xr", [P, 3, D])
        scr = sb("scr", [P, NT])
        zp = sb("zp", [P, G, PS + T])
        zps = sb("zps", [P, G, NS, PS + TS])
        zc = sb("zc", [P, G, CS + T])
        zcs = sb("zcs", [P, G, NS, CS + TS])
        tree = sb("tree", [P, 2, PS + T])
        trees = sb("trees", [P, 2, NS, PS + TS])
        gt1 = sb("gt1", [P, D])
        gt1s = sb("gt1s", [S, D])
        ct = sb("ct", [P, KC, NR])
        prow = sb("prow", [28, P])
        cwrow = sb("cwrow", [CK * G, P])
        par = sb("par", [P, 28])
        cw = sb("cw", [P, CK, G])
        bi, cb, lg, lb, psc = par[:, 0:12], par[:, 12:16], par[:, 16:20], par[:, 20:24], par[:, 24:28]
        sprow = sb("sprow", [NS * PS, GW])
        scrow = sb("scrow", [NS * CS // 2, 2, GW])
        modt = sb("modt", [P, 2, KC, NR])
        wp = sb("wp", [P, G, P])
        inv = sb("inv", [P, G, 16])
        ones1 = sb("ones1", [1, P])
        new_rows = sb("new_rows", [P, 2, G, S])
        mean_w = sb("mean_w", [P, P])
        ss = sb("ss", [P, NB + 1])
        std = sb("std", [P, NB + 1])
        rstd = sb("rstd", [P, NB + 1])

        c_in, par_in, g_in, wp_in, bout_in = (sem(n) for n in ("c_in", "par_in", "g_in", "wp_in", "bout_in"))
        ada_in = [sem(f"ada_in{i}") for i in range(3)]
        x_in = [sem(f"x_in{i}") for i in range(3)]
        w_in_in, w_out_in, gt1_in = sem("w_in_in"), sem("w_out_in"), sem("gt1_in")
        const_ready, csil_ready, ct_ps, ct_ready = sem("const_ready"), sem("csil_ready"), sem("ct_ps"), sem("ct_ready")
        par_ps, par_ready = sem("par_ps"), sem("par_ready")
        mod_ps, mod_taken, modrow_ready, modt_ps, modt_ready = (
            sem(n) for n in ("mod_ps", "mod_taken", "modrow_ready", "modt_ps", "modt_ready"))
        mod_stored = sem("mod_stored")
        ss_ready, std_ready, xn_ready, xt_ps, h1_ready = (
            sem(n) for n in ("ss_ready", "std_ready", "xn_ready", "xt_ps", "h1_ready"))
        proj_ps, act_taken, glu_done = sem("proj_ps"), sem("act_taken"), sem("glu_done")
        diff_ready, pool_ps, pool_ready = sem("diff_ready"), sem("pool_ps"), sem("pool_ready")
        new_ready = sem("new_ready")
        conv_done, st_ps, st_ready, st_stored = sem("conv_done"), sem("st_ps"), sem("st_ready"), sem("st_stored")
        mean_ps, xc_ready, sq_ready, var_ps, lnstd_ready, yn_ready, cm_ready = (
            sem(n) for n in ("mean_ps", "xc_ready", "sq_ready", "var_ps", "lnstd_ready", "yn_ready", "cm_ready"))
        mix_ps, x1_ready = sem("mix_ps"), sem("x1_ready")
        x1_stored = [sem(f"x1_stored{i}") for i in range(3)]

        block = ctx.enter_context(nc.Block())

        def rows(i):
            return P if i < NB else S

        def x_rows(i):
            return x_prompt[0, i * P:(i + 1) * P, :] if i < NB else x_sample.rearrange("b t d -> (b t) d")

        @block.sync
        def _(sp):
            sp.dma_start(csil[0:1, :], c_prompt).then_inc(c_in, 16)
            sp.dma_start(csil[1:NR, :], c_sample).then_inc(c_in, 16)
            w_ada_v = w_ada[0].rearrange("(k p) n -> p k n", p=P)
            for n in range(12):
                if n == 1:
                    for row, n_rows, src in ((0, 12, b_in), (12, 4, conv_b), (16, 4, ln_g), (20, 4, ln_b), (24, 4, pool_scale)):
                        sp.dma_start(prow[row:row + n_rows, :], src[0].rearrange("(c p) -> c p", p=P)).then_inc(par_in, 16)
                    sp.dma_start(cwrow[:, :], conv_w[0, :, 0, :].rearrange("j (c p) -> (j c) p", p=P)).then_inc(par_in, 16)
                    sp.dma_start(sprow[:, :], state_pool[0].rearrange("b s n -> (b s) n")).then_inc(par_in, 16)
                    sp.dma_start(scrow[:, :, :], state_conv[0].rearrange("(h b) s n -> (b s) h n", h=2)).then_inc(par_in, 16)
                    sp.dma_start(g1row, g_norm1.broadcast_to([NR, D])).then_inc(g_in, 16)
                    sp.dma_start(g2row, g_norm2.broadcast_to([NR, D])).then_inc(g_in, 16)
                    sp.dma_start(wp[:, :, :], w_pool[0].rearrange("g c d -> c g d")).then_inc(wp_in, 16)
                if n >= 3:
                    sp.wait_ge(mod_ps, n - 2)
                sp.dma_start(ada[:, n % 3], w_ada_v[:, :, n * HALF:(n + 1) * HALF]).then_inc(ada_in[n % 3], 16)
                sp.dma_start(ada_b[:, n % 3], b_ada[:, n * HALF:(n + 1) * HALF]).then_inc(ada_in[n % 3], 16)
            for i in range(3):
                sp.dma_start(xr[0:rows(i), i % 3], x_rows(i)).then_inc(x_in[i % 3], 16)
            sp.wait_ge(mod_ps, 12)
            sp.dma_start(win, w_in[0].rearrange("(k p) n -> p k n", p=P)).then_inc(w_in_in, 16)
            sp.wait_ge(modrow_ready, 1)
            sp.dma_start(mod_dram, modrow).then_inc(mod_stored, 16)
            for i in range(3, NB + 1):
                sp.wait_ge(xt_ps, i - 2)
                sp.dma_start(xr[0:rows(i), i % 3], x_rows(i)).then_inc(x_in[i % 3], 16)
            sp.wait_ge(mod_stored, 16)
            sp.dma_start(gt1[:, :], mod_dram[0:1, GT1 * D:(GT1 + 1) * D].broadcast_to([P, D])).then_inc(gt1_in, 16)
            for r in range(NS):
                sp.dma_start(gt1s[r * TS:(r + 1) * TS, :], mod_dram[1 + r:2 + r, GT1 * D:(GT1 + 1) * D].broadcast_to([TS, D])).then_inc(gt1_in, 16)
            sp.dma_start(pool_sample[0, :, 0:PS - TS, :], state_pool[0, :, TS:PS, :]).then_inc(st_stored, 16)
            sp.dma_start(conv_sample[0, :, 0:CS - TS, :], state_conv[0, :, TS:CS, :]).then_inc(st_stored, 16)
            for i in range(3):
                sp.wait_ge(xt_ps, NB - 1 + i)
                sp.dma_start(xr[0:rows(i), i % 3], x_rows(i)).then_inc(x_in[i % 3], 16)
            sp.wait_ge(proj_ps, 12)
            sp.dma_start(wout, w_out[0].rearrange("(k p) n -> p k n", p=P)).then_inc(w_out_in, 16)
            sp.dma_start(bout, b_out).then_inc(bout_in, 16)
            sp.wait_ge(st_ready, 4)
            sp.dma_start(pool_prompt[0, 0], st_out[0:PS, 0]).then_inc(st_stored, 16)
            sp.dma_start(conv_prompt[0, 0], st_out[0:CS, 1]).then_inc(st_stored, 16)
            for b in range(NS):
                sp.dma_start(pool_sample[0, b, PS - TS:PS, :], st_out[b * TS:(b + 1) * TS, 2]).then_inc(st_stored, 16)
                sp.dma_start(conv_sample[0, b, CS - TS:CS, :], st_out[b * TS:(b + 1) * TS, 3]).then_inc(st_stored, 16)
            for i in range(NB + 1):
                sp.wait_ge(x1_ready, i + 1)
                sp.dma_start(x1_dram[i * P:i * P + rows(i), :], xr[0:rows(i), i % 3]).then_inc(x1_stored[i % 3], 16)
                if i + 3 <= NB:
                    sp.wait_ge(x1_stored[i % 3], 16 * (i // 3 + 1))
                    sp.dma_start(xr[0:rows(i + 3), i % 3], x_rows(i + 3)).then_inc(x_in[i % 3], 16)
            for i in range(3):
                sp.wait_ge(x1_stored[i], 16 * 3)
            sp.wait_ge(st_stored, 16 * (4 + 2 * NS))

        @block.gpsimd
        def _(pool):
            pool.memset(ident[:, :], 0.0)
            pool.drain()
            pool.affine_select(out=ident[:, :], in_=ident[:, :], compare_op=ALU.not_equal, fill=1.0, base=0,
                               pattern=[[-1, P]], channel_multiplier=1)
            pool.memset(eps_c[:, :], EPS)
            pool.memset(ones1[:, :], 1.0)
            pool.memset(mean_w[:, :], 1.0 / GW)
            pool.memset(zp[:, :, 0:PS], 0.0)
            pool.memset(zc[:, :, 0:CS], 0.0)
            for g, w in enumerate(WIN):
                for t in range(16):
                    pool.memset(inv[:, g, t:t + 1], 1.0 / min(t + 1, w))
            pool.drain().then_inc(const_ready, 1)
            pool.wait_ge(par_ready, 1)
            for g, w in enumerate(WIN):
                pool.wait_ge(act_taken, 2 * g + 2)
                src, srcs, step = zp[:, g], zps[:, g], 1
                for lvl in range(g + 1):
                    dst, dsts, lo = tree[:, lvl % 2], trees[:, lvl % 2], 2 * step - 1
                    pool.tensor_tensor(dst[:, lo:PS + T], src[:, lo:PS + T], src[:, lo - step:PS + T - step], ALU.add)
                    pool.tensor_tensor(dsts[:, :, lo:PS + TS], srcs[:, :, lo:PS + TS],
                                       srcs[:, :, lo - step:PS + TS - step], ALU.add)
                    pool.drain()
                    src, srcs, step = dst, dsts, 2 * step
                pool.tensor_tensor(mixt[:, g, 0:16], src[:, PS:PS + 16], inv[:, g], ALU.mult)
                pool.tensor_scalar(mixt[:, g, 16:T], src[:, PS + 16:PS + T], 1.0 / w, 1.0, ALU.mult, ALU.mult)
                out_s = mixt[:, g, T:NT].rearrange("p (b t) -> p b t", b=NS)
                pool.tensor_scalar(out_s, srcs[:, :, PS:PS + TS], 1.0 / w, 1.0, ALU.mult, ALU.mult)
                pool.drain()
                pool.tensor_tensor(mixt[:, g, 0:T], mixt[:, g, 0:T], zp[:, g, PS:PS + T], ALU.subtract)
                pool.tensor_tensor(out_s, out_s, zps[:, g, :, PS:PS + TS], ALU.subtract)
                pool.drain().then_inc(diff_ready, 1)
            pool.wait_ge(glu_done, G)
            for a, (z, n) in enumerate(((zps, PS), (zcs, CS))):
                for g in range(G):
                    pool.tensor_copy(new_rows[:, a, g].rearrange("p (b t) -> p b t", b=NS), z[:, g, :, n:n + TS])
            pool.drain().then_inc(new_ready, 1)

        @block.scalar
        def _(act):
            act.wait_ge(c_in, 32)
            act.activation(csil, csil, ACT.Silu).then_inc(csil_ready, 1)
            act.wait_ge(const_ready, 1)
            for i in range(NB + 1):
                n = rows(i)
                act.wait_ge(ss_ready, i + 1)
                act.activation(std[0:n, i:i + 1], ss[0:n, i:i + 1], ACT.Sqrt, bias=eps_c[0:n, :], scale=1.0 / D).then_inc(std_ready, 1)
                if i < NB:
                    act.wait_ge(modt_ready, 1)
                    act.wait_ge(xt_ps, i + 1)
                    for k in range(KC):
                        last = act.activation(h1t[:, k, i * P:(i + 1) * P],
                                              ps[2 + 2 * (i % 2) + k // 4][:, k % 4 * P:(k % 4 + 1) * P],
                                              ACT.Identity, bias=modt[:, 0, k, 0:1], scale=modt[:, 1, k, 0:1])
                    last.then_inc(h1_ready, 1)
            for c in range(G):
                act.wait_ge(proj_ps, 3 * c + 1)
                if c:
                    act.wait_ge(glu_done, c)
                for r, (t0, n) in enumerate(REG):
                    last = act.activation(scr[:, t0:t0 + n], ps[3 * (3 * c % 2) + r][:, 0:n], ACT.Sigmoid,
                                          bias=bi[:, 8 + c:9 + c])
                last.then_inc(act_taken, 1)
                act.wait_ge(proj_ps, 3 * c + 3)
                bank = 3 * ((3 * c + 2) % 2)
                for r in range(2):
                    act.activation(zp[:, c, PS + r * HALF:PS + (r + 1) * HALF], ps[bank + r][:, :], ACT.Identity,
                                   bias=bi[:, c:c + 1])
                act.activation(zps[:, c, :, PS:PS + TS], ps[bank + 2][:, 0:S].rearrange("p (b t) -> p b t", b=NS),
                               ACT.Identity, bias=bi[:, c:c + 1])
                act.drain().then_inc(act_taken, 1)
            for g in range(G):
                act.wait_ge(pool_ps, g + 1)
                for r, (t0, n) in enumerate(REG):
                    last = act.activation(mixt[:, g, t0:t0 + n], ps[3 * (g % 2) + r][:, 0:n], ACT.Copy, scale=psc[:, g:g + 1])
                last.then_inc(pool_ready, 1)
            for s in range(4):
                act.wait_ge(st_ps, s + 1)
                n = (PS, CS, S, S)[s]
                act.activation(st_out[0:n, s], ps[6 + s % 2][0:n, :], ACT.Copy).then_inc(st_ready, 1)
            act.wait_ge(xc_ready, 1)
            for c in range(G):
                last = act.activation(sq[:, c], mixt[:, G + c], ACT.Square)
            last.then_inc(sq_ready, 1)
            act.wait_ge(var_ps, 1)
            for r, (t0, n) in enumerate(REG):
                last = act.activation(rstd_ln[:, t0:t0 + n], ps[3 + r][:, 0:n], ACT.Sqrt, bias=eps_c[:, :])
            last.then_inc(lnstd_ready, 1)
            for c in range(G):
                act.wait_ge(yn_ready, c + 1)
                act.activation(mixt[:, G + c], mixt[:, G + c], ACT.Silu, bias=lb[:, c:c + 1], scale=lg[:, c:c + 1]).then_inc(cm_ready, 1)

        @block.vector
        def _(dve):
            dve.wait_ge(ct_ps, 1)
            dve.tensor_copy(ct[:, :, :], ps[0][:, 0:KC * NR].rearrange("p (k r) -> p k r", k=KC)).then_inc(ct_ready, 1)
            dve.wait_ge(par_ps, 1)
            dve.tensor_copy(par[:, :], ps[1][:, 0:28])
            dve.tensor_copy(cw[:, :, :], ps[1][:, P:P + CK * G].rearrange("p (j c) -> p j c", c=G))
            for g in range(G):
                dve.tensor_copy(zps[:, g, :, 0:PS], ps[2][:, g * NS * PS:(g + 1) * NS * PS].rearrange("p (b s) -> p b s", s=PS))
                for h in range(2):
                    n = NS * CS // 2
                    dve.tensor_copy(zcs[:, g, h * 4:h * 4 + 4, 0:CS], ps[3 + h][:, g * n:(g + 1) * n].rearrange("p (b s) -> p b s", s=CS))
            dve.drain().then_inc(par_ready, 1)
            for n in range(12):
                dve.wait_ge(mod_ps, n + 1)
                dve.tensor_copy(modrow[:, n * HALF:(n + 1) * HALF], ps[5 + n % 3][0:NR, :]).then_inc(mod_taken, 1)
            dve.drain()
            dve.wait_ge(g_in, 32)
            for col, grow in ((SC1, g1row), (SC2, g2row)):
                part = modrow[:, col * D:(col + 1) * D]
                last = dve.scalar_tensor_tensor(out=part, in0=part, scalar=1.0, in1=grow, op0=ALU.add, op1=ALU.mult)
            dve.drain().then_inc(modrow_ready, 1)
            dve.wait_ge(modt_ps, 1)
            dve.tensor_copy(modt[:, :, :, :], ps[1][:, 0:2 * KC * NR].rearrange("p (a k r) -> p a k r", a=2, k=KC)).then_inc(modt_ready, 1)

            def squares(i):
                n = rows(i)
                dve.wait_ge(x_in[i % 3], 16 * (i // 3 + 1))
                dve.tensor_tensor_reduce(scr[0:n, 0:D], xr[0:n, i % 3], xr[0:n, i % 3], 1.0, 0.0, ALU.mult, ALU.add,
                                         ss[0:n, i:i + 1]).then_inc(ss_ready, 1)

            squares(0)
            for i in range(NB + 1):
                n = rows(i)
                dve.drain()
                if i < NB:
                    squares(i + 1)
                dve.wait_ge(std_ready, i + 1)
                dve.reciprocal(rstd[0:n, i:i + 1], std[0:n, i:i + 1])
                dve.drain()
                dve.tensor_scalar(xr[0:n, i % 3], xr[0:n, i % 3], rstd[0:n, i:i + 1], None, ALU.mult).then_inc(xn_ready, 1)
            dve.wait_ge(xt_ps, NB + 1)
            shape = [P, KC, NS, TS]
            hs = h1t[:, :, T:NT].rearrange("p k (b t) -> p k b t", b=NS)
            xs = ps[2][:, 0:KC * S].rearrange("p (k b t) -> p k b t", k=KC, b=NS)
            dve.tensor_tensor(hs, xs, modt[:, 1, :, 1:NR].unsqueeze(3).broadcast_to(shape), ALU.mult)
            dve.drain()
            dve.tensor_tensor(hs, hs, modt[:, 0, :, 1:NR].unsqueeze(3).broadcast_to(shape), ALU.add).then_inc(h1_ready, 1)
            for c in range(G):
                dve.wait_ge(proj_ps, 3 * c + 2)
                dve.wait_ge(act_taken, 2 * c + 1)
                bank = 3 * ((3 * c + 1) % 2)
                for r in range(2):
                    dve.scalar_tensor_tensor(out=zc[:, c, CS + r * HALF:CS + (r + 1) * HALF], in0=ps[bank + r][:, :],
                                             scalar=bi[:, 4 + c:5 + c], in1=scr[:, r * HALF:(r + 1) * HALF],
                                             op0=ALU.add, op1=ALU.mult)
                dve.scalar_tensor_tensor(out=zcs[:, c, :, CS:CS + TS], in0=ps[bank + 2][:, 0:S].rearrange("p (b t) -> p b t", b=NS),
                                         scalar=bi[:, 4 + c:5 + c], in1=scr[:, T:NT].rearrange("p (b t) -> p b t", b=NS),
                                         op0=ALU.add, op1=ALU.mult)
                dve.drain().then_inc(glu_done, 1)
                out_p = mixt[:, G + c, 0:T]
                out_s = mixt[:, G + c, T:NT].rearrange("p (b t) -> p b t", b=NS)
                dve.tensor_scalar(out_p, zc[:, c, 0:T], cw[:, 0, c:c + 1], cb[:, c:c + 1], ALU.mult, ALU.add)
                dve.tensor_scalar(out_s, zcs[:, c, :, 0:TS], cw[:, 0, c:c + 1], cb[:, c:c + 1], ALU.mult, ALU.add)
                for j in range(1, CK):
                    dve.drain()
                    dve.scalar_tensor_tensor(out=out_p, in0=zc[:, c, j:j + T], scalar=cw[:, j, c:c + 1], in1=out_p,
                                             op0=ALU.mult, op1=ALU.add)
                    dve.scalar_tensor_tensor(out=out_s, in0=zcs[:, c, :, j:j + TS], scalar=cw[:, j, c:c + 1], in1=out_s,
                                             op0=ALU.mult, op1=ALU.add)
                dve.drain().then_inc(conv_done, 1)
            dve.wait_ge(mean_ps, 1)
            for c in range(G):
                for r, (t0, n) in enumerate(REG):
                    dve.tensor_tensor(mixt[:, G + c, t0:t0 + n], mixt[:, G + c, t0:t0 + n], ps[r][:, 0:n], ALU.subtract)
            dve.drain().then_inc(xc_ready, 1)
            dve.wait_ge(lnstd_ready, 1)
            dve.reciprocal(rstd_ln, rstd_ln)
            dve.drain()
            dve.wait_ge(sq_ready, 1)
            for c in range(G):
                dve.tensor_tensor(mixt[:, G + c], mixt[:, G + c], rstd_ln, ALU.mult).then_inc(yn_ready, 1)
            dve.wait_ge(gt1_in, 16 * (1 + NS))
            for i in range(NB + 1):
                n = rows(i)
                dve.wait_ge(mix_ps, i + 1)
                dve.wait_ge(x_in[i % 3], 16 * (3 + i // 3 + 1))
                g = gt1 if i < NB else gt1s
                for h in range(2):
                    dve.tensor_tensor(scr[0:n, h * HALF:(h + 1) * HALF], ps[2 * (i % 3) + h][0:n, :], g[0:n, h * HALF:(h + 1) * HALF], ALU.mult)
                dve.drain()
                dve.tensor_tensor(xr[0:n, i % 3], xr[0:n, i % 3], scr[0:n, 0:D], ALU.add).then_inc(x1_ready, 1)
                dve.drain()

        @block.tensor
        def _(pe):
            pe.wait_ge(const_ready, 1)
            pe.wait_ge(csil_ready, 1)
            for k in range(KC):
                last = pe.transpose(ps[0][:, k * NR:(k + 1) * NR], csil[:, k * P:(k + 1) * P], ident[0:NR, 0:NR])
            last.then_inc(ct_ps, 1)
            pe.wait_ge(par_in, 16 * 8)
            pe.transpose(ps[1][:, 0:28], prow[:, :], ident[0:28, 0:28])
            pe.transpose(ps[1][:, P:P + CK * G], cwrow[:, :], ident[0:CK * G, 0:CK * G])
            for g in range(G):
                n = NS * PS
                pe.transpose(ps[2][:, g * n:(g + 1) * n], sprow[:, g * P:(g + 1) * P], ident[0:n, 0:n])
                for h in range(2):
                    last = pe.transpose(ps[3 + h][:, g * n:(g + 1) * n], scrow[:, h, g * P:(g + 1) * P], ident[0:n, 0:n])
            last.then_inc(par_ps, 1)
            pe.wait_ge(ct_ready, 1)
            for n in range(12):
                pe.wait_ge(ada_in[n % 3], 32 * (n // 3 + 1))
                if n >= 3:
                    pe.wait_ge(mod_taken, n - 2)
                bank = ps[5 + n % 3][0:NR, :]
                pe.matmul(bank, ones1[0:1, 0:NR], ada_b[0:1, n % 3], start=True, stop=False)
                for k in range(KC):
                    last = pe.matmul(bank, ct[:, k, :], ada[:, n % 3, k], start=False, stop=(k == KC - 1))
                last.then_inc(mod_ps, 1)
            pe.wait_ge(modrow_ready, 1)
            pe.wait_ge(par_ready, 1)
            for a, col in enumerate((SH1, SC1)):
                for k in range(KC):
                    last = pe.transpose(ps[1][:, (a * KC + k) * NR:(a * KC + k + 1) * NR],
                                        modrow[:, col * D + k * P:col * D + (k + 1) * P], ident[0:NR, 0:NR])
            last.then_inc(modt_ps, 1)
            for i in range(NB + 1):
                n = rows(i)
                pe.wait_ge(xn_ready, i + 1)
                if i >= 2:
                    pe.wait_ge(h1_ready, i - 1)
                for k in range(KC):
                    out = ps[2 + 2 * (i % 2) + k // 4][:, k % 4 * P:(k % 4 + 1) * P] if i < NB else ps[2][:, k * S:(k + 1) * S]
                    last = pe.transpose(out, xr[0:n, i % 3, k * P:(k + 1) * P], ident[0:n, 0:n])
                last.then_inc(xt_ps, 1)
            pe.wait_ge(w_in_in, 16)
            pe.wait_ge(h1_ready, NB + 1)
            for c in range(G):
                for t, n in enumerate((8 + c, 4 + c, c)):
                    m = 3 * c + t
                    if c and t == 0:
                        pe.wait_ge(glu_done, c)
                    if t == 1 and c:
                        pe.wait_ge(act_taken, 2 * c)
                    if t == 2:
                        pe.wait_ge(act_taken, 2 * c + 1)
                    for k in range(KC):
                        for r, (t0, w) in enumerate(REG):
                            last = pe.matmul(ps[3 * (m % 2) + r][:, 0:w], win[:, k, n * P:(n + 1) * P], h1t[:, k, t0:t0 + w],
                                             start=(k == 0), stop=(k == KC - 1))
                    last.then_inc(proj_ps, 1)
            pe.wait_ge(wp_in, 16)
            pe.wait_ge(glu_done, G)
            pe.wait_ge(act_taken, 2 * G)
            for g in range(G):
                pe.wait_ge(diff_ready, g + 1)
                if g >= 2:
                    pe.wait_ge(pool_ready, g - 1)
                for r, (t0, w) in enumerate(REG):
                    last = pe.matmul(ps[3 * (g % 2) + r][:, 0:w], wp[:, g, :], mixt[:, g, t0:t0 + w], start=True, stop=True)
                last.then_inc(pool_ps, 1)
            for s in range(4):
                if s >= 2:
                    pe.wait_ge(st_ready, s - 1)
                if s == 2:
                    pe.wait_ge(new_ready, 1)
                for g in range(G):
                    src = (zp[:, g, T:T + PS], zc[:, g, T:T + CS], new_rows[:, 0, g], new_rows[:, 1, g])[s]
                    n = (PS, CS, S, S)[s]
                    last = pe.transpose(ps[6 + s % 2][0:n, g * P:(g + 1) * P], src, ident[:, :])
                last.then_inc(st_ps, 1)
            pe.wait_ge(conv_done, G)
            pe.wait_ge(pool_ready, G)
            for r, (t0, w) in enumerate(REG):
                for c in range(G):
                    last = pe.matmul(ps[r][:, 0:w], mean_w[:, :], mixt[:, G + c, t0:t0 + w], start=(c == 0), stop=(c == G - 1))
            last.then_inc(mean_ps, 1)
            pe.wait_ge(sq_ready, 1)
            for r, (t0, w) in enumerate(REG):
                for c in range(G):
                    last = pe.matmul(ps[3 + r][:, 0:w], mean_w[:, :], sq[:, c, t0:t0 + w], start=(c == 0), stop=(c == G - 1))
            last.then_inc(var_ps, 1)
            pe.wait_ge(w_out_in, 16)
            pe.wait_ge(bout_in, 16)
            pe.wait_ge(lnstd_ready, 1)
            pe.wait_ge(cm_ready, G)
            for i in range(NB + 1):
                n = rows(i)
                if i >= 3:
                    pe.wait_ge(x1_ready, i - 2)
                for h in range(2):
                    bank = ps[2 * (i % 3) + h][0:n, :]
                    pe.matmul(bank, ones1[0:1, 0:n], bout[:, h * HALF:(h + 1) * HALF], start=True, stop=False)
                    for k in range(KC):
                        last = pe.matmul(bank, mixt[:, k, i * P:i * P + n], wout[:, k, h * HALF:(h + 1) * HALF],
                                         start=False, stop=(k == KC - 1))
                last.then_inc(mix_ps, 1)


def expert_phase(nc, ps, ident, eps_c, x1_dram, mod_dram, w_query, sub_keys, u_table, v_table, g_final,
                 y_prompt, y_sample):
    with ExitStack() as ctx:
        def sb(name, shape, dt=F32):
            return ctx.enter_context(nc.sbuf_tensor(name, shape, dt))

        def sem(name):
            return ctx.enter_context(nc.semaphore(name))

        wq = sb("wq", [P, KC, 2 * H * P])
        keyt = sb("keyt", [P, 2 * H, NKEY])
        u_ring = sb("u_ring", [P, RING, D])
        v_ring = sb("v_ring", [P, RING, D])
        krow = v_ring[:, 0:2, :].rearrange("p a (b k) -> p (a b) k", k=P)
        mod2 = sb("mod2", [P, 3, D])
        gfin = sb("gfin", [P, D])
        x1 = sb("x1", [P, D])
        h2n = sb("h2n", [P, D])
        h2c = sb("h2c", [P, D])
        y = sb("y", [P, D])
        scratch = sb("scratch", [P, D])
        h2t = sb("h2t", [P, KC, P])
        qt = sb("qt", [P, 4, P])
        s_sb = sb("s_sb", [P, 4, NKEY])
        s_rep = sb("s_rep", [P, NKEY])
        sv = sb("sv", [P, 4, K])
        si = sb("si", [P, 4, K], U32)
        sif = sb("sif", [P, 4, K])
        comb = sb("comb", [P, K * K])
        comb_rep = sb("comb_rep", [P, K * K])
        fpos = sb("fpos", [P, 2, K], U32)
        fhalf = sb("fhalf", [P, 2, 2 * K], U32)
        fhalff = sb("fhalff", [P, 2, 2 * K])
        hot = sb("hot", [P, 2, K, K])
        keyno = sb("keyno", [P, 2, 2, K])
        iota = sb("iota", [P, K])
        fv = sb("fv", [P, H, K])
        fsum = sb("fsum", [P, H])
        gaten = sb("gaten", [P, H, K])
        gatec = sb("gatec", [P, H, K])
        eidf = sb("eidf", [P, H * K])
        eidn = sb("eidn", [P, H * K], U32)
        eidc = sb("eidc", [P, H * K], U32)
        none = sb("none", [P, H * K], U32)
        mark = sb("mark", [1, 1])
        sel = sb("sel", [P, P])
        dot = sb("dot", [P, K])
        gel = sb("gel", [P, K])
        act_w = sb("act_w", [P, K])
        diag = sb("diag", [P, RING, P])
        zeros = sb("zeros", [1, HALF], BF16)
        st = sb("st", [P, 6])

        wq_in, key_in, mod2_in, gfin_in, x1_in, y_in = (sem(n) for n in ("wq_in", "key_in", "mod2_in", "gfin_in", "x1_in", "y_in"))
        u_in = [sem(f"u_in{i}") for i in range(RING)]
        v_in = [sem(f"v_in{i}") for i in range(RING)]
        u_free, v_free, dot_free, dot_ready, gel_done, diag_ready = (
            sem(n) for n in ("u_free", "v_free", "dot_free", "dot_ready", "gel_done", "diag_ready"))
        const2, key_ps, key_ready = sem("const2"), sem("key_ps"), sem("key_ready")
        ss_done, std_done, h2_ready, h2_ps, h2t_ready = (sem(n) for n in ("ss_done", "std_done", "h2_ready", "h2_ps", "h2t_ready"))
        q_ps, qt_ready, s_ps, s_taken = sem("q_ps"), sem("qt_ready"), sem("s_ps"), sem("s_taken")
        turns, eid_low = sem("turns"), sem("eid_low")
        top_ready, exp_ready, found, eid_taken, cur_ready, gate_used = (
            sem(n) for n in ("top_ready", "exp_ready", "found", "eid_taken", "cur_ready", "gate_used"))
        acc_ready, acc_free, fin_ss, fin_std, y_ready, y_stored = (
            sem(n) for n in ("acc_ready", "acc_free", "fin_ss", "fin_std", "y_ready", "y_stored"))

        u_rows, v_rows = u_table[0], v_table[0]
        acc = ps[0:2]
        S2, A2, GT = range(3)
        LAST = NB - 1
        NCH = H * CPH

        block = ctx.enter_context(nc.Block())


        @block.sync
        def _(sp):
            sp.dma_start(krow, sub_keys[0].rearrange("h p m k -> m (h p) k")).then_inc(key_in, 16)
            sp.dma_start(x1[:, :], x1_dram[0:P, :]).then_inc(x1_in, 16)
            for a, col in enumerate((SH2, SC2, GT2)):
                sp.dma_start(mod2[:, a], mod_dram[0:1, col * D:(col + 1) * D].broadcast_to([P, D])).then_inc(mod2_in, 16)
            for q in range(4):
                sp.dma_start(wq[:, :, q * HALF:(q + 1) * HALF],
                             w_query[0, :, q * HALF:(q + 1) * HALF].rearrange("(k p) n -> p k n", p=P)).then_inc(wq_in, 16)
            sp.dma_start(gfin[:, :], g_final.rearrange("(a d) -> a d", a=1).broadcast_to([P, D])).then_inc(gfin_in, 16)
            sp.dma_start(y[:, :], x1_dram[0:P, :]).then_inc(y_in, 16)

            def rest(b, src_next, dst):
                sp.wait_ge(y_ready, b + 1)
                sp.dma_start(dst, y[:, :]).then_inc(y_stored, 16)
                sp.wait_ge(y_stored, (b + 1) * 16)
                sp.dma_start(y[:, :], src_next).then_inc(y_in, 16)

            with sp.Fori(0, LAST) as b:
                sp.wait_ge(h2_ready, b + 1)
                sp.dma_start(x1[:, :], x1_dram[bass.ds((b + 1) * P, P), :]).then_inc(x1_in, 16)
                rest(b, x1_dram[bass.ds((b + 1) * P, P), :], y_prompt[0, bass.ds(b * P, P), :])
            sp.wait_ge(h2_ready, LAST + 1)
            for q in range(4):
                sp.dma_start(x1[q * S:(q + 1) * S, :], x1_dram[T:NT, :]).then_inc(x1_in, 16)
                for r in range(NS):
                    p0 = q * S + r * TS
                    for a, col in enumerate((SH2, SC2)):
                        sp.dma_start(mod2[p0:p0 + TS, a], mod_dram[1 + r:2 + r, col * D:(col + 1) * D].broadcast_to([TS, D])).then_inc(mod2_in, 16)
            sp.wait_ge(y_ready, LAST + 1)
            sp.dma_start(y_prompt[0, LAST * P:T, :], y[:, :]).then_inc(y_stored, 16)
            sp.wait_ge(y_stored, (LAST + 1) * 16)
            for q in range(4):
                sp.dma_start(y[q * S:(q + 1) * S, :], x1_dram[T:NT, :]).then_inc(y_in, 16)
                for r in range(NS):
                    p0 = q * S + r * TS
                    sp.dma_start(mod2[p0:p0 + TS, GT], mod_dram[1 + r:2 + r, GT2 * D:(GT2 + 1) * D].broadcast_to([TS, D])).then_inc(mod2_in, 16)
            sp.wait_ge(y_ready, NB + 1)
            sp.dma_start(y_sample.rearrange("b t d -> (b t) d"), y[0:S, :]).then_inc(y_stored, 16)
            sp.wait_ge(y_stored, (NB + 1) * 16)

        @block.gpsimd
        def _(pool):
            pool.memset(sel[:, :], 0.0)
            pool.memset(zeros[:, :], 0.0)
            pool.memset(none[:, :], 0)
            for k in range(K):
                pool.memset(iota[:, k:k + 1], float(k))
            for q in range(-3, 4):
                pool.drain()
                pool.affine_select(out=sel[:, :], in_=sel[:, :], compare_op=ALU.not_equal, fill=1.0, base=q * S,
                                   pattern=[[-1, P]], channel_multiplier=1)
            pool.drain().then_inc(const2, 1)
            pool.drain().then_inc(turns, 1)

            def turn(n, ready, count):
                pool.wait_ge(turns, n + 1)
                pool.wait_ge(ready, count)
                pool.tensor_tensor(mark[:, :], iota[0:1, 0:1], iota[0:1, 1:2], ALU.add).then_inc(turns, 1)

            def chunk(n, c):
                for a, (ring, landed, free, table) in enumerate(((u_ring, u_in, u_free, u_rows), (v_ring, v_in, v_free, v_rows))):
                    turn(2 * n + a, free, n + 1)
                    for j in range(CH):
                        slot = c % 2 * CH + j
                        pool.indirect_dma_start(ring[:, slot], None, table,
                                                bass.IndirectOffsetOnAxis(ap=eidc[:, c * CH + j:c * CH + j + 1], axis=0)
                                                ).then_inc(landed[slot], 16)

            def gathers(b):
                half = H * K // 2
                pool.wait_ge(found, b + 1)
                pool.tensor_tensor(eidc[:, 0:half], eidn[:, 0:half], none[:, 0:half], ALU.add).then_inc(eid_low, 1)
                pool.wait_ge(eid_low, b + 1)
                for c in range(NCH):
                    if c == CPH:
                        pool.wait_ge(turns, 2 * (b * NCH + c) + 1)
                        pool.tensor_tensor(eidc[:, half:], eidn[:, half:], none[:, half:], ALU.add).then_inc(eid_taken, 1)
                        pool.wait_ge(eid_taken, b + 1)
                    chunk(b * NCH + c, c)

            with pool.Fori(0, LAST) as b:
                gathers(b)
            gathers(LAST)
            pool.wait_ge(found, NB + 1)
            for slot in range(CH, RING):
                pool.wait_ge(v_in[slot], 16 * (NB * NCH // 2))
            for q in range(4):
                last = pool.tensor_copy(eidc[q * S:(q + 1) * S, 0:2 * K], eidn[q * S:(q + 1) * S, q * 2 * K:(q + 1) * 2 * K])
            pool.drain()
            for c in range(2 * CPH):
                chunk(NB * NCH + c, c)

        @block.scalar
        def _(act):
            act.wait_ge(key_ps, 1)
            for i in range(4):
                last = act.activation(keyt[:, 4 * i:4 * i + 4, :], ps[2 + i][:, :].rearrange("p (a m) -> p a m", a=4), ACT.Copy)
            last.then_inc(key_ready, 1)

            def root(f, col, ready, done):
                act.wait_ge(ready, f + 1)
                act.activation(st[:, col + 1:col + 2], st[:, col:col + 1], ACT.Sqrt, bias=eps_c[:, :], scale=1.0 / D).then_inc(done, 1)

            def norm(f):
                root(f, 0, ss_done, std_done)
                act.wait_ge(h2_ps, f + 1)
                for i in range(2):
                    last = act.activation(h2t[:, 4 * i:4 * i + 4, :], ps[2 + i][:, :].rearrange("p (a t) -> p a t", a=4), ACT.Copy)
                last.then_inc(h2t_ready, 1)

            def query(f, part):
                act.wait_ge(q_ps, f * FE_PARTS + part + 1)
                act.activation(qt[:, :, :], ps[4][:, :].rearrange("p (a t) -> p a t", a=4), ACT.Copy).then_inc(qt_ready, 1)

            def softmax(f):
                act.wait_ge(top_ready, f + 1)
                act.activation(gaten[:, :, :], gaten[:, :, :], ACT.Exp).then_inc(exp_ready, 1)

            def chunk(n, c, fold):
                c0 = c % CPH * CH
                act.wait_ge(dot_ready, n + 1)
                act.activation(gel[:, c0:c0 + CH], dot[:, c0:c0 + CH], ACT.Gelu).then_inc(dot_free, 1)
                act.drain()
                gate = gatec[:, :, :].rearrange("p h k -> p (h k)")
                for j in range(CH):
                    act.activation(act_w[:, c0 + j:c0 + j + 1], gel[:, c0 + j:c0 + j + 1], ACT.Copy,
                                   scale=gate[:, c * CH + j:c * CH + j + 1])
                act.drain()
                act.wait_ge(v_free, n + 1)
                for j in range(CH):
                    last = act.activation(diag[:, c % 2 * CH + j, :], fold[:, :], ACT.Copy, scale=act_w[:, c0 + j:c0 + j + 1])
                last.then_inc(diag_ready, 1)

            def block_steps(b, retrieve):
                f = b + 1
                for h in range(H if retrieve else 2):
                    if retrieve:
                        if h == 0:
                            norm(f)
                            query(f, 0)
                        if h in (2, 4, 5):
                            query(f, {2: 1, 4: 2, 5: 3}[h])
                        if h == H - 1:
                            softmax(f)
                    if h == 0:
                        act.wait_ge(cur_ready, b + 1)
                    for c in range(h * CPH, (h + 1) * CPH):
                        chunk(b * NCH + c, c, ident if retrieve else sel)
                act.drain().then_inc(gate_used, 1)
                root(b, 3, fin_ss, fin_std)

            norm(0)
            for part in range(FE_PARTS):
                query(0, part)
            softmax(0)
            with act.Fori(0, LAST) as b:
                block_steps(b, True)
            block_steps(LAST, True)
            act.wait_ge(const2, 1)
            block_steps(NB, False)

        @block.vector
        def _(dve):
            dve.drain().then_inc(u_free, 2)
            dve.drain().then_inc(v_free, 2)
            dve.drain().then_inc(dot_free, CPH)
            dve.drain().then_inc(acc_free, 1)
            dve.drain().then_inc(gate_used, 1)
            dve.wait_ge(const2, 1)

            def norm(f):
                dve.wait_ge(x1_in, 16 * (f + 1) if not (isinstance(f, int) and f == NB) else 16 * (NB + 4))
                dve.tensor_tensor_reduce(scratch[:, :], x1[:, :], x1[:, :], 1.0, 0.0, ALU.mult, ALU.add, st[:, 0:1]).then_inc(ss_done, 1)
                dve.wait_ge(std_done, f + 1)
                dve.reciprocal(st[:, 2:3], st[:, 1:2])
                dve.drain()
                dve.scalar_tensor_tensor(out=h2n[:, :], in0=x1[:, :], scalar=st[:, 2:3], in1=mod2[:, A2], op0=ALU.mult, op1=ALU.mult)
                dve.drain()
                dve.tensor_tensor(h2n[:, :], h2n[:, :], mod2[:, S2], ALU.add).then_inc(h2_ready, 1)

            def top16(vals, idx, src, rep):
                dve.max(vals[:, 0:8], src)
                dve.drain()
                dve.match_replace(rep, vals[:, 0:8], src, -3.0e38)
                dve.max_index(idx[:, 0:8], vals[:, 0:8], src)
                dve.drain()
                dve.max(vals[:, 8:16], rep)
                dve.drain()
                dve.max_index(idx[:, 8:16], vals[:, 8:16], rep)

            def retrieve(f, part):
                dve.wait_ge(s_ps, f * FE_PARTS + part + 1)
                dve.tensor_copy(s_sb[:, :, :], ps[5][:, :].rearrange("p (a m) -> p a m", a=4)).then_inc(s_taken, 1)
                dve.drain()
                for i in range(4):
                    top16(sv[:, i], si[:, i], s_sb[:, i], s_rep[:, :])
                    dve.drain()
                dve.tensor_copy(sif[:, :, :], si[:, :, :])
                for j in range(2):
                    c3 = comb[:, :].rearrange("p (a b) -> p a b", a=K)
                    dve.tensor_tensor(c3, sv[:, 2 * j].unsqueeze(2).broadcast_to([P, K, K]),
                                      sv[:, 2 * j + 1].unsqueeze(1).broadcast_to([P, K, K]), ALU.add)
                    dve.drain()
                    top16(fv[:, 2 * part + j], fpos[:, j], comb[:, :], comb_rep[:, :])
                    dve.drain()
                dve.tensor_scalar(fhalf[:, :, 0:K], fpos[:, :, :], 4, None, ALU.logical_shift_right)
                dve.tensor_scalar(fhalf[:, :, K:2 * K], fpos[:, :, :], K - 1, None, ALU.bitwise_and)
                dve.drain()
                dve.tensor_copy(fhalff[:, :, :], fhalf[:, :, :])
                for a in range(2):
                    shape = [P, 2, K, K]
                    dve.drain()
                    dve.tensor_tensor(hot[:, :, :, :], fhalff[:, :, a * K:(a + 1) * K].unsqueeze(3).broadcast_to(shape),
                                      iota[:, :].unsqueeze(1).unsqueeze(1).broadcast_to(shape), ALU.is_equal)
                    dve.drain()
                    dve.tensor_tensor(hot[:, :, :, :], hot[:, :, :, :],
                                      sif[:, a:4:2, :].unsqueeze(2).broadcast_to(shape), ALU.mult)
                    dve.drain()
                    dve.tensor_reduce(keyno[:, a], hot[:, :, :, :], AX, ALU.add)
                dve.drain()
                dve.scalar_tensor_tensor(out=eidf[:, part * 2 * K:(part + 1) * 2 * K].rearrange("p (a k) -> p a k", a=2),
                                         in0=keyno[:, 0], scalar=float(NKEY), in1=keyno[:, 1], op0=ALU.mult, op1=ALU.add)

            def finish_retrieval(f, first):
                dve.drain()
                dve.tensor_tensor(gaten[:, :, :], fv[:, :, :], fv[:, :, 0:1].broadcast_to([P, H, K]), ALU.subtract).then_inc(top_ready, 1)
                dve.wait_ge(exp_ready, f + 1)
                dve.tensor_reduce(fsum[:, :], gaten[:, :, :], AX, ALU.add)
                dve.drain()
                dve.reciprocal(fsum[:, :], fsum[:, :])
                dve.drain()
                dve.tensor_tensor(gaten[:, :, :], gaten[:, :, :], fsum[:, :].unsqueeze(2).broadcast_to([P, H, K]), ALU.mult)
                if not first:
                    dve.wait_ge(eid_taken, f)
                dve.tensor_copy(eidn[:, :], eidf[:, :])
                dve.drain().then_inc(found, 1)

            def chunk(n, c, r):
                c0 = c % CPH * CH
                dve.wait_ge(dot_free, n + 1)
                for j in range(CH):
                    slot = c % 2 * CH + j
                    dve.wait_ge(u_in[slot], 16 * (r + 1))
                    last = dve.tensor_tensor_reduce(u_ring[:, slot], u_ring[:, slot], h2c[:, :], 1.0, 0.0, ALU.mult, ALU.add,
                                                    dot[:, c0 + j:c0 + j + 1])
                dve.drain().then_inc(dot_ready, 1)
                dve.drain().then_inc(u_free, 1)

            def block_steps(b, prompt):
                f = b + 1
                dve.wait_ge(gate_used, b + 1)
                dve.tensor_copy(h2c[:, :], h2n[:, :])
                if prompt:
                    dve.tensor_copy(gatec[:, :, :], gaten[:, :, :])
                else:
                    for q in range(4):
                        dve.tensor_copy(gatec[q * S:(q + 1) * S, 0:2, :], gaten[q * S:(q + 1) * S, 2 * q:2 * q + 2, :])
                dve.drain().then_inc(cur_ready, 1)
                for h in range(H if prompt else 2):
                    if prompt:
                        if h == 0:
                            if isinstance(b, int):
                                dve.wait_ge(mod2_in, 16 * (3 + 4 * NS * 2))
                            norm(f)
                        if h in (1, 3, 5, 6):
                            retrieve(f, {1: 0, 3: 1, 5: 2, 6: 3}[h])
                        if h == H - 1:
                            finish_retrieval(f, False)
                    for c in range(h * CPH, (h + 1) * CPH):
                        chunk(b * NCH + c, c, b * (NCH // 2) + c // 2)
                dve.wait_ge(acc_ready, b + 1)
                if not prompt:
                    dve.wait_ge(mod2_in, 16 * (3 + 4 * NS * 3))
                for i in range(2):
                    dve.tensor_tensor(scratch[:, i * HALF:(i + 1) * HALF], acc[i][:, :], mod2[:, GT, i * HALF:(i + 1) * HALF], ALU.mult)
                dve.drain().then_inc(acc_free, 1)
                dve.wait_ge(y_in, 16 * (b + 1) if prompt else 16 * (NB + 4))
                dve.tensor_tensor(y[:, :], y[:, :], scratch[:, :], ALU.add)
                dve.drain()
                dve.tensor_tensor_reduce(scratch[:, :], y[:, :], y[:, :], 1.0, 0.0, ALU.mult, ALU.add, st[:, 3:4]).then_inc(fin_ss, 1)
                dve.wait_ge(fin_std, b + 1)
                dve.reciprocal(st[:, 5:6], st[:, 4:5])
                dve.drain()
                dve.scalar_tensor_tensor(out=y[:, :], in0=y[:, :], scalar=st[:, 5:6], in1=gfin[:, :], op0=ALU.mult, op1=ALU.mult).then_inc(y_ready, 1)
                dve.drain()

            dve.wait_ge(mod2_in, 16 * 3)
            norm(0)
            for part in range(FE_PARTS):
                retrieve(0, part)
            finish_retrieval(0, True)
            dve.wait_ge(gfin_in, 16)
            with dve.Fori(0, LAST) as b:
                block_steps(b, True)
            block_steps(LAST, True)
            block_steps(NB, False)

        @block.tensor
        def _(pe):
            pe.wait_ge(key_in, 16)
            for i in range(2 * H):
                last = pe.transpose(ps[2 + i // 4][:, i % 4 * P:(i % 4 + 1) * P], krow[:, i, :], ident[:, :])
            last.then_inc(key_ps, 1)
            pe.wait_ge(key_ready, 1)

            def norm(f):
                pe.wait_ge(h2_ready, f + 1)
                for k in range(KC):
                    last = pe.transpose(ps[2 + k // 4][:, k % 4 * P:(k % 4 + 1) * P], h2n[:, k * P:(k + 1) * P], ident[:, :])
                last.then_inc(h2_ps, 1)
                pe.wait_ge(h2t_ready, f + 1)

            def query(f, part):
                for i in range(4):
                    for k in range(KC):
                        last = pe.matmul(ps[4][:, i * P:(i + 1) * P], wq[:, k, (part * 4 + i) * P:(part * 4 + i + 1) * P], h2t[:, k, :],
                                         start=(k == 0), stop=(k == KC - 1))
                last.then_inc(q_ps, 1)
                pe.wait_ge(qt_ready, f * FE_PARTS + part + 1)
                pe.wait_ge(s_taken, f * FE_PARTS + part)
                for i in range(4):
                    last = pe.matmul(ps[5][:, i * P:(i + 1) * P], qt[:, i, :], keyt[:, part * 4 + i, :], start=True, stop=True)
                last.then_inc(s_ps, 1)

            def zero(start):
                for i in range(2):
                    last = pe.matmul(acc[i][:, :], zeros[0:1, 0:P], zeros[0:1, :], start=start, stop=not start, skip_group_check=True)
                return last

            def chunk(n, c, r):
                pe.wait_ge(diag_ready, n + 1)
                for j in range(CH):
                    slot = c % 2 * CH + j
                    pe.wait_ge(v_in[slot], 16 * (r + 1))
                    for i in range(2):
                        last = pe.matmul(acc[i][:, :], diag[:, slot, :], v_ring[:, slot, i * HALF:(i + 1) * HALF],
                                         start=False, stop=False, skip_group_check=True)
                last.then_inc(v_free, 1)

            def block_steps(b, prompt):
                f = b + 1
                for h in range(H if prompt else 2):
                    if prompt:
                        if h == 0:
                            norm(f)
                            query(f, 0)
                        if h in (2, 4, 5):
                            query(f, {2: 1, 4: 2, 5: 3}[h])
                    if h == 0:
                        pe.wait_ge(acc_free, b + 1)
                        zero(True)
                    for c in range(h * CPH, (h + 1) * CPH):
                        chunk(b * NCH + c, c, b * (NCH // 2) + c // 2)
                zero(False).then_inc(acc_ready, 1)

            pe.wait_ge(wq_in, 16 * 4)
            pe.wait_ge(const2, 1)
            norm(0)
            for part in range(FE_PARTS):
                query(0, part)
            with pe.Fori(0, LAST) as b:
                block_steps(b, True)
            block_steps(LAST, True)
            block_steps(NB, False)


_INS = ['x_prompt', 'x_sample', 'state_pool', 'state_conv', 'c_prompt', 'c_sample', 'w_ada', 'b_ada', 'g_norm1', 'g_norm2',
        'w_in', 'b_in', 'w_pool', 'pool_scale', 'conv_w', 'conv_b', 'ln_g', 'ln_b', 'w_out', 'b_out', 'w_query', 'sub_keys',
        'u_table', 'v_table', 'g_final']
_OUTS = [(1, T, D), (NS, TS, D), (1, 1, PS, GW), (1, 1, CS, GW), (1, NS, PS, GW), (1, NS, CS, GW)]


def kernel(**inputs):
    import numpy as _np
    import concourse.bacc as _bacc
    from concourse import mybir as _mybir
    from concourse.bass_utils import run_bass_kernel_spmd as _run

    nc = _bacc.Bacc("TRN2", target_bir_lowering=False, num_devices=1)
    arrays, args = {}, []
    for name in _INS:
        a = _np.ascontiguousarray(inputs[name])
        arrays[f"in_{name}_dram"] = a
        args.append(nc.dram_tensor(f"in_{name}_dram", a.shape, _mybir.dt.from_np(a.dtype), kind="ExternalInput").ap())
    for i, shape in enumerate(_OUTS):
        args.append(nc.dram_tensor(f"out_{i}_dram", shape, _mybir.dt.float32, kind="ExternalOutput").ap())
    build(nc, *args)
    r = _run(nc, [arrays], core_ids=[0])
    return tuple(r.results[0][f"out_{i}_dram"] for i in range(len(_OUTS)))
```

```python
from contextlib import ExitStack

import concourse.bass as bass
from concourse import mybir

F32 = mybir.dt.float32
BF16 = mybir.dt.bfloat16
U32 = mybir.dt.uint32
ALU = mybir.AluOpType
ACT = mybir.ActivationFunctionType
AX = mybir.AxisListType.X

P = 128
D = 1024
KC = D // P
T = 1024
NB = T // P
NS = 8
TS = 4
S = NS * TS
NT = T + S
NR = 1 + NS
NMOD = 6
G = 4
WIN = [2, 4, 8, 16]
PS = 15
CK = 31
CS = CK - 1
GW = G * P
EPS = 1e-6
H = 8
K = 16
NKEY = 128
HALF = 512
CH = 4
RING = 2 * CH
CPH = K // CH
SH1, SC1, GT1, SH2, SC2, GT2 = range(NMOD)
REG = [(0, HALF), (HALF, HALF), (T, S)]
PARTS = 4
PK = H * K // PARTS
PIECES = 6


def build(nc, x_prompt, x_sample, state_pool, state_conv, c_prompt, c_sample, w_ada, b_ada, g_norm1, g_norm2,
          w_in, b_in, w_pool, pool_scale, conv_w, conv_b, ln_g, ln_b, w_out, b_out, w_query, sub_keys,
          u_table, v_table, g_final, y_prompt, y_sample, pool_prompt, conv_prompt, pool_sample, conv_sample):
    x1_dram = nc.dram_tensor("x1_scratch", [NT, D], F32, kind="Internal").ap()
    mod_dram = nc.dram_tensor("mod_scratch", [NR, NMOD * D], F32, kind="Internal").ap()
    with ExitStack() as ctx:
        ps = [ctx.enter_context(nc.psum_tensor(f"bank{i}", [P, HALF], F32)) for i in range(8)]
        ident = ctx.enter_context(nc.sbuf_tensor("ident", [P, P], F32))
        eps_c = ctx.enter_context(nc.sbuf_tensor("eps_c", [P, 1], F32))
        wq = ctx.enter_context(nc.sbuf_tensor("wq", [P, PARTS, KC, HALF], F32))
        wq_in = [ctx.enter_context(nc.semaphore(f"wq_in{i}")) for i in range(PARTS)]
        mixer_phase(nc, ps, ident, eps_c, wq, wq_in, w_query, x1_dram, mod_dram, x_prompt, x_sample, state_pool, state_conv, c_prompt,
                    c_sample, w_ada, b_ada, g_norm1, g_norm2, w_in, b_in, w_pool, pool_scale, conv_w, conv_b,
                    ln_g, ln_b, w_out, b_out, pool_prompt, conv_prompt, pool_sample, conv_sample)
        expert_phase(nc, ps, ident, eps_c, wq, wq_in, x1_dram, mod_dram, sub_keys, u_table, v_table, g_final,
                     y_prompt, y_sample)


def mixer_phase(nc, ps, ident, eps_c, wq, wq_in, w_query, x1_dram, mod_dram, x_prompt, x_sample, state_pool, state_conv, c_prompt,
                c_sample, w_ada, b_ada, g_norm1, g_norm2, w_in, b_in, w_pool, pool_scale, conv_w, conv_b,
                ln_g, ln_b, w_out, b_out, pool_prompt, conv_prompt, pool_sample, conv_sample):
    with ExitStack() as ctx:
        def sb(name, shape, dt=F32):
            return ctx.enter_context(nc.sbuf_tensor(name, shape, dt))

        def sem(name):
            return ctx.enter_context(nc.semaphore(name))

        wbuf = sb("wbuf", [P, 3 * KC * HALF])
        ada = wbuf[:, :].rearrange("p (r k n) -> p r k n", r=3, k=KC)
        win = wbuf[:, :].rearrange("p (k n) -> p k n", k=KC)
        wout = wbuf[:, 0:KC * D].rearrange("p (k n) -> p k n", k=KC)
        bout = wbuf[0:1, KC * D:KC * D + D]
        gt1 = wbuf[:, KC * D + D + NT:KC * D + 2 * D + NT]
        rstd_ln = wbuf[:, KC * D + D:KC * D + D + NT]
        ada_b = sb("ada_b", [1, 3, HALF])
        h1t = sb("h1t", [P, KC, NT])
        flat = h1t[:, :, :].rearrange("p k t -> p (k t)")
        csil = flat[0:NR, 0:D]
        sq = flat[:, 0:G * NT].rearrange("p (c t) -> p c t", c=G)
        st_out = flat[0:S, G * NT:G * NT + 4 * GW].rearrange("p (s n) -> p s n", s=4)
        mixt = sb("mixt", [P, 2 * G, NT])
        mflat = mixt[:, :, :].rearrange("p k t -> p (k t)")
        modrow = mflat[0:NR, 0:NMOD * D]
        g1row = mflat[0:NR, NMOD * D:(NMOD + 1) * D]
        g2row = mflat[0:NR, (NMOD + 1) * D:(NMOD + 2) * D]
        prow = mflat[0:28, (NMOD + 2) * D:(NMOD + 2) * D + P]
        cwrow = mflat[0:CK * G, (NMOD + 2) * D + P:(NMOD + 2) * D + 2 * P]
        xr = sb("xr", [P, 3, D])
        scr = sb("scr", [P, NT])
        wqflat = wq[:, :, :, :].rearrange("p a k n -> p (a k n)")
        at = 0

        def share(*shape):
            nonlocal at
            n = 1
            for x in shape:
                n *= x
            at += n
            names = " ".join("abc"[:len(shape)])
            return wqflat[:, at - n:at].rearrange(f"p ({names}) -> p {names}", **dict(zip("abc", shape)))

        zp, zps = share(G, PS + T), share(G, NS, PS + TS)
        zc, zcs = share(G, CS + T), share(G, NS, CS + TS)
        tree, trees = share(2, PS + T), share(2, NS, PS + TS)
        sprow, scrow, wp = share(GW)[0:NS * PS], share(2, GW)[0:NS * CS // 2], share(G, P)
        new_rows = share(2, G * S).rearrange("p a (g t) -> p a g t", g=G)
        inv = share(G, 16)
        gt1s = sb("gt1s", [S, D])
        ct = sb("ct", [P, KC, NR])
        par = sb("par", [P, 28])
        cw = sb("cw", [P, CK, G])
        bi, cb, lg, lb, psc = par[:, 0:12], par[:, 12:16], par[:, 16:20], par[:, 20:24], par[:, 24:28]
        modt = sb("modt", [P, 2, KC, NR])
        ones1 = sb("ones1", [1, P])
        mean_w = sb("mean_w", [P, P])
        ss = sb("ss", [P, NB + 1])
        std = sb("std", [P, NB + 1])
        rstd = sb("rstd", [P, NB + 1])

        c_in, par_in, g_in, wp_in, bout_in = (sem(n) for n in ("c_in", "par_in", "g_in", "wp_in", "bout_in"))
        ada_in = [sem(f"ada_in{i}") for i in range(3)]
        x_in = [sem(f"x_in{i}") for i in range(3)]
        w_in_in, w_out_in, gt1_in = sem("w_in_in"), sem("w_out_in"), sem("gt1_in")
        const_ready, csil_ready, ct_ps, ct_ready = sem("const_ready"), sem("csil_ready"), sem("ct_ps"), sem("ct_ready")
        par_ps, par_ready = sem("par_ps"), sem("par_ready")
        mod_ps, mod_taken, modrow_ready, modt_ps, modt_ready = (
            sem(n) for n in ("mod_ps", "mod_taken", "modrow_ready", "modt_ps", "modt_ready"))
        mod_stored = sem("mod_stored")
        ss_ready, std_ready, xn_ready, xt_ps, h1_ready = (
            sem(n) for n in ("ss_ready", "std_ready", "xn_ready", "xt_ps", "h1_ready"))
        proj_ps, act_taken, glu_done = sem("proj_ps"), sem("act_taken"), sem("glu_done")
        diff_ready, pool_ps, pool_ready = sem("diff_ready"), sem("pool_ps"), sem("pool_ready")
        new_ready = sem("new_ready")
        conv_done, st_ps, st_ready, st_stored = sem("conv_done"), sem("st_ps"), sem("st_ready"), sem("st_stored")
        mean_ps, xc_ready, sq_ready, var_ps, lnstd_ready, yn_ready, cm_ready = (
            sem(n) for n in ("mean_ps", "xc_ready", "sq_ready", "var_ps", "lnstd_ready", "yn_ready", "cm_ready"))
        mix_ps, x1_ready, xt_taken = sem("mix_ps"), sem("x1_ready"), sem("xt_taken")
        XB = ((2, 3), (4, 0))
        OB = ((6, 7), (0, 1), (2, 3))
        x1_stored = [sem(f"x1_stored{i}") for i in range(3)]

        block = ctx.enter_context(nc.Block())

        def rows(i):
            return P if i < NB else S

        def x_rows(i):
            return x_prompt[0, i * P:(i + 1) * P, :] if i < NB else x_sample.rearrange("b t d -> (b t) d")

        @block.sync
        def _(sp):
            sp.dma_start(csil[0:1, :], c_prompt).then_inc(c_in, 16)
            sp.dma_start(csil[1:NR, :], c_sample).then_inc(c_in, 16)
            w_ada_v = w_ada[0].rearrange("(k p) n -> p k n", p=P)
            for n in range(12):
                if n == 1:
                    for row, n_rows, src in ((0, 12, b_in), (12, 4, conv_b), (16, 4, ln_g), (20, 4, ln_b), (24, 4, pool_scale)):
                        sp.dma_start(prow[row:row + n_rows, :], src[0].rearrange("(c p) -> c p", p=P)).then_inc(par_in, 16)
                    sp.dma_start(cwrow[:, :], conv_w[0, :, 0, :].rearrange("j (c p) -> (j c) p", p=P)).then_inc(par_in, 16)
                    sp.dma_start(sprow[:, :], state_pool[0].rearrange("b s n -> (b s) n")).then_inc(par_in, 16)
                    sp.dma_start(scrow[:, :, :], state_conv[0].rearrange("(h b) s n -> (b s) h n", h=2)).then_inc(par_in, 16)
                    sp.dma_start(g1row, g_norm1.broadcast_to([NR, D])).then_inc(g_in, 16)
                    sp.dma_start(g2row, g_norm2.broadcast_to([NR, D])).then_inc(g_in, 16)
                    sp.dma_start(wp[:, :, :], w_pool[0].rearrange("g c d -> c g d")).then_inc(wp_in, 16)
                    for i in range(3):
                        sp.dma_start(xr[0:rows(i), i % 3], x_rows(i)).then_inc(x_in[i % 3], 16)
                if n >= 3:
                    sp.wait_ge(mod_ps, n - 2)
                sp.dma_start(ada[:, n % 3], w_ada_v[:, :, n * HALF:(n + 1) * HALF]).then_inc(ada_in[n % 3], 16)
                sp.dma_start(ada_b[:, n % 3], b_ada[:, n * HALF:(n + 1) * HALF]).then_inc(ada_in[n % 3], 16)
                if 4 <= n < 10:
                    i = n - 1
                    sp.wait_ge(xt_ps, i - 2)
                    sp.dma_start(xr[0:rows(i), i % 3], x_rows(i)).then_inc(x_in[i % 3], 16)
            w_in_v = w_in[0].rearrange("(k p) n -> p k n", p=P)
            for ready, k0, k1 in ((10, 0, 2), (11, 2, 5), (12, 5, KC)):
                sp.wait_ge(mod_ps, ready)
                sp.dma_start(win[:, k0:k1], w_in_v[:, k0:k1]).then_inc(w_in_in, 16)
            sp.wait_ge(modrow_ready, 1)
            sp.dma_start(mod_dram, modrow).then_inc(mod_stored, 16)
            sp.dma_start(pool_sample[0, :, 0:PS - TS, :], state_pool[0, :, TS:PS, :]).then_inc(st_stored, 16)
            sp.dma_start(conv_sample[0, :, 0:CS - TS, :], state_conv[0, :, TS:CS, :]).then_inc(st_stored, 16)
            for i in range(3):
                sp.wait_ge(xt_ps, NB - 1 + i)
                sp.dma_start(xr[0:rows(i), i % 3], x_rows(i)).then_inc(x_in[i % 3], 16)
            sp.wait_ge(proj_ps, 12)
            sp.dma_start(wout, w_out[0].rearrange("(k p) n -> p k n", p=P)).then_inc(w_out_in, 16)
            sp.dma_start(bout, b_out).then_inc(bout_in, 16)
            sp.wait_ge(mod_stored, 16)
            sp.dma_start(gt1[:, :], mod_dram[0:1, GT1 * D:(GT1 + 1) * D].broadcast_to([P, D])).then_inc(gt1_in, 16)
            for r in range(NS):
                sp.dma_start(gt1s[r * TS:(r + 1) * TS, :], mod_dram[1 + r:2 + r, GT1 * D:(GT1 + 1) * D].broadcast_to([TS, D])).then_inc(gt1_in, 16)
            sp.wait_ge(conv_done, G)
            sp.wait_ge(st_ps, 4)
            for q in range(PARTS):
                sp.dma_start(wq[:, q], w_query[0, :, q * HALF:(q + 1) * HALF].rearrange("(k p) n -> p k n", p=P)).then_inc(wq_in[q], 16)
            sp.wait_ge(st_ready, 4)
            sp.dma_start(pool_prompt[0, 0], st_out[0:PS, 0]).then_inc(st_stored, 16)
            sp.dma_start(conv_prompt[0, 0], st_out[0:CS, 1]).then_inc(st_stored, 16)
            for b in range(NS):
                sp.dma_start(pool_sample[0, b, PS - TS:PS, :], st_out[b * TS:(b + 1) * TS, 2]).then_inc(st_stored, 16)
                sp.dma_start(conv_sample[0, b, CS - TS:CS, :], st_out[b * TS:(b + 1) * TS, 3]).then_inc(st_stored, 16)
            for i in range(NB + 1):
                sp.wait_ge(x1_ready, i + 1)
                sp.dma_start(x1_dram[i * P:i * P + rows(i), :], xr[0:rows(i), i % 3]).then_inc(x1_stored[i % 3], 16)
                if i + 3 <= NB:
                    sp.wait_ge(x1_stored[i % 3], 16 * (i // 3 + 1))
                    sp.dma_start(xr[0:rows(i + 3), i % 3], x_rows(i + 3)).then_inc(x_in[i % 3], 16)
            for i in range(3):
                sp.wait_ge(x1_stored[i], 16 * 3)
            sp.wait_ge(st_stored, 16 * (4 + 2 * NS))

        @block.gpsimd
        def _(pool):
            pool.memset(ident[:, :], 0.0)
            pool.drain()
            pool.affine_select(out=ident[:, :], in_=ident[:, :], compare_op=ALU.not_equal, fill=1.0, base=0,
                               pattern=[[-1, P]], channel_multiplier=1)
            pool.memset(eps_c[:, :], EPS)
            pool.memset(ones1[:, :], 1.0)
            pool.memset(mean_w[:, :], 1.0 / GW)
            pool.memset(zp[:, :, 0:PS], 0.0)
            pool.memset(zc[:, :, 0:CS], 0.0)
            for g, w in enumerate(WIN):
                for t in range(16):
                    pool.memset(inv[:, g, t:t + 1], 1.0 / min(t + 1, w))
            pool.drain().then_inc(const_ready, 1)
            pool.wait_ge(par_ready, 1)
            pool.wait_ge(mod_stored, 16)
            for g, w in enumerate(WIN):
                pool.wait_ge(act_taken, 2 * g + 2)
                src, srcs, step = zp[:, g], zps[:, g], 1
                for lvl in range(g + 1):
                    dst, dsts, lo = tree[:, lvl % 2], trees[:, lvl % 2], 2 * step - 1
                    pool.tensor_tensor(dst[:, lo:PS + T], src[:, lo:PS + T], src[:, lo - step:PS + T - step], ALU.add)
                    pool.tensor_tensor(dsts[:, :, lo:PS + TS], srcs[:, :, lo:PS + TS],
                                       srcs[:, :, lo - step:PS + TS - step], ALU.add)
                    pool.drain()
                    src, srcs, step = dst, dsts, 2 * step
                pool.tensor_tensor(mixt[:, g, 0:16], src[:, PS:PS + 16], inv[:, g], ALU.mult)
                pool.tensor_scalar(mixt[:, g, 16:T], src[:, PS + 16:PS + T], 1.0 / w, 1.0, ALU.mult, ALU.mult)
                out_s = mixt[:, g, T:NT].rearrange("p (b t) -> p b t", b=NS)
                pool.tensor_scalar(out_s, srcs[:, :, PS:PS + TS], 1.0 / w, 1.0, ALU.mult, ALU.mult)
                pool.drain()
                pool.tensor_tensor(mixt[:, g, 0:T], mixt[:, g, 0:T], zp[:, g, PS:PS + T], ALU.subtract)
                pool.tensor_tensor(out_s, out_s, zps[:, g, :, PS:PS + TS], ALU.subtract)
                pool.drain().then_inc(diff_ready, 1)
            pool.wait_ge(glu_done, G)
            for a, (z, n) in enumerate(((zps, PS), (zcs, CS))):
                for g in range(G):
                    pool.tensor_copy(new_rows[:, a, g].rearrange("p (b t) -> p b t", b=NS), z[:, g, :, n:n + TS])
            pool.drain().then_inc(new_ready, 1)

        @block.scalar
        def _(act):
            act.wait_ge(c_in, 32)
            act.activation(csil, csil, ACT.Silu).then_inc(csil_ready, 1)
            act.wait_ge(const_ready, 1)
            def x_evac(i):
                act.wait_ge(xt_ps, i + 1)
                for h in range(2):
                    if i < NB:
                        last = act.activation(h1t[:, 4 * h:4 * h + 4, i * P:(i + 1) * P],
                                              ps[XB[i % 2][h]][:, :].rearrange("p (k t) -> p k t", k=4), ACT.Copy)
                    elif h == 0:
                        last = act.activation(h1t[:, :, T:NT], ps[XB[0][0]][:, 0:KC * S].rearrange("p (k t) -> p k t", k=KC), ACT.Copy)
                last.then_inc(xt_taken, 1)

            for i in range(NB + 1):
                n = rows(i)
                act.wait_ge(ss_ready, i + 1)
                act.activation(std[0:n, i:i + 1], ss[0:n, i:i + 1], ACT.Sqrt, bias=eps_c[0:n, :], scale=1.0 / D).then_inc(std_ready, 1)
                if i:
                    x_evac(i - 1)
            x_evac(NB)
            for c in range(G):
                act.wait_ge(proj_ps, 3 * c + 1)
                if c:
                    act.wait_ge(glu_done, c)
                for r, (t0, n) in enumerate(REG):
                    last = act.activation(scr[:, t0:t0 + n], ps[3 * (3 * c % 2) + r][:, 0:n], ACT.Sigmoid,
                                          bias=bi[:, 8 + c:9 + c])
                last.then_inc(act_taken, 1)
                act.wait_ge(proj_ps, 3 * c + 3)
                bank = 3 * ((3 * c + 2) % 2)
                for r in range(2):
                    act.activation(zp[:, c, PS + r * HALF:PS + (r + 1) * HALF], ps[bank + r][:, :], ACT.Identity,
                                   bias=bi[:, c:c + 1])
                act.activation(zps[:, c, :, PS:PS + TS], ps[bank + 2][:, 0:S].rearrange("p (b t) -> p b t", b=NS),
                               ACT.Identity, bias=bi[:, c:c + 1])
                act.drain().then_inc(act_taken, 1)
            for g in range(G):
                act.wait_ge(pool_ps, g + 1)
                for r, (t0, n) in enumerate(REG):
                    last = act.activation(mixt[:, g, t0:t0 + n], ps[3 * (g % 2) + r][:, 0:n], ACT.Copy, scale=psc[:, g:g + 1])
                last.then_inc(pool_ready, 1)
            for s in range(4):
                act.wait_ge(st_ps, s + 1)
                n = (PS, CS, S, S)[s]
                act.activation(st_out[0:n, s], ps[6 + s % 2][0:n, :], ACT.Copy).then_inc(st_ready, 1)
            for r, (t0, n) in enumerate(REG):
                act.wait_ge(xc_ready, r + 1)
                act.activation(sq[:, :, t0:t0 + n], mixt[:, G:2 * G, t0:t0 + n], ACT.Square).then_inc(sq_ready, 1)
            for r, (t0, n) in enumerate(REG):
                act.wait_ge(var_ps, r + 1)
                act.activation(rstd_ln[:, t0:t0 + n], ps[3 + r][:, 0:n], ACT.Sqrt, bias=eps_c[:, :]).then_inc(lnstd_ready, 1)
            for r, (t0, n) in enumerate(REG):
                act.wait_ge(yn_ready, r + 1)
                for c in range(G):
                    m = mixt[:, G + c, t0:t0 + n]
                    last = act.activation(m, m, ACT.Silu, bias=lb[:, c:c + 1], scale=lg[:, c:c + 1])
                last.then_inc(cm_ready, 1)

        @block.vector
        def _(dve):
            dve.wait_ge(ct_ps, 1)
            dve.tensor_copy(ct[:, :, :], ps[0][:, 0:KC * NR].rearrange("p (k r) -> p k r", k=KC)).then_inc(ct_ready, 1)
            dve.wait_ge(par_ps, 1)
            dve.tensor_copy(par[:, :], ps[1][:, 0:28])
            dve.tensor_copy(cw[:, :, :], ps[1][:, P:P + CK * G].rearrange("p (j c) -> p j c", c=G))
            for g in range(G):
                dve.tensor_copy(zps[:, g, :, 0:PS], ps[2][:, g * NS * PS:(g + 1) * NS * PS].rearrange("p (b s) -> p b s", s=PS))
                for h in range(2):
                    n = NS * CS // 2
                    dve.tensor_copy(zcs[:, g, h * 4:h * 4 + 4, 0:CS], ps[3 + h][:, g * n:(g + 1) * n].rearrange("p (b s) -> p b s", s=CS))
            dve.drain().then_inc(par_ready, 1)
            def squares(i):
                n = rows(i)
                dve.wait_ge(x_in[i % 3], 16 * (i // 3 + 1))
                dve.tensor_tensor_reduce(scr[0:n, 0:D], xr[0:n, i % 3], xr[0:n, i % 3], 1.0, 0.0, ALU.mult, ALU.add,
                                         ss[0:n, i:i + 1]).then_inc(ss_ready, 1)
                dve.drain()

            def normed(i):
                n = rows(i)
                dve.wait_ge(std_ready, i + 1)
                dve.reciprocal(rstd[0:n, i:i + 1], std[0:n, i:i + 1])
                dve.drain()
                dve.tensor_scalar(xr[0:n, i % 3], xr[0:n, i % 3], rstd[0:n, i:i + 1], None, ALU.mult).then_inc(xn_ready, 1)

            for n in range(12):
                dve.wait_ge(mod_ps, n + 1)
                dve.tensor_copy(modrow[:, n * HALF:(n + 1) * HALF], ps[5 + n % 3][0:NR, :]).then_inc(mod_taken, 1)
                if 1 <= n <= NB + 1:
                    squares(n - 1)
                if 2 <= n <= NB + 2:
                    normed(n - 2)
            dve.drain()
            dve.wait_ge(g_in, 32)
            for col, grow in ((SC1, g1row), (SC2, g2row)):
                part = modrow[:, col * D:(col + 1) * D]
                last = dve.scalar_tensor_tensor(out=part, in0=part, scalar=1.0, in1=grow, op0=ALU.add, op1=ALU.mult)
            dve.drain().then_inc(modrow_ready, 1)
            dve.wait_ge(modt_ps, 1)
            dve.tensor_copy(modt[:, :, :, :], ps[1][:, 0:2 * KC * NR].rearrange("p (a k r) -> p a k r", a=2, k=KC))
            dve.drain()
            dve.wait_ge(xt_taken, NB + 1)
            for k in range(KC):
                dve.tensor_scalar(h1t[:, k, 0:T], h1t[:, k, 0:T], modt[:, 1, k, 0:1], modt[:, 0, k, 0:1], ALU.mult, ALU.add)
            shape = [P, KC, NS, TS]
            hs = h1t[:, :, T:NT].rearrange("p k (b t) -> p k b t", b=NS)
            dve.tensor_tensor(hs, hs, modt[:, 1, :, 1:NR].unsqueeze(3).broadcast_to(shape), ALU.mult)
            dve.drain()
            dve.tensor_tensor(hs, hs, modt[:, 0, :, 1:NR].unsqueeze(3).broadcast_to(shape), ALU.add)
            dve.drain().then_inc(h1_ready, 1)
            for c in range(G):
                dve.wait_ge(proj_ps, 3 * c + 2)
                dve.wait_ge(act_taken, 2 * c + 1)
                bank = 3 * ((3 * c + 1) % 2)
                for r in range(2):
                    dve.scalar_tensor_tensor(out=zc[:, c, CS + r * HALF:CS + (r + 1) * HALF], in0=ps[bank + r][:, :],
                                             scalar=bi[:, 4 + c:5 + c], in1=scr[:, r * HALF:(r + 1) * HALF],
                                             op0=ALU.add, op1=ALU.mult)
                dve.scalar_tensor_tensor(out=zcs[:, c, :, CS:CS + TS], in0=ps[bank + 2][:, 0:S].rearrange("p (b t) -> p b t", b=NS),
                                         scalar=bi[:, 4 + c:5 + c], in1=scr[:, T:NT].rearrange("p (b t) -> p b t", b=NS),
                                         op0=ALU.add, op1=ALU.mult)
                dve.drain().then_inc(glu_done, 1)
                if c == 0:
                    dve.wait_ge(mod_stored, 16)
                out_p = mixt[:, G + c, 0:T]
                out_s = mixt[:, G + c, T:NT].rearrange("p (b t) -> p b t", b=NS)
                dve.tensor_scalar(out_p, zc[:, c, 0:T], cw[:, 0, c:c + 1], cb[:, c:c + 1], ALU.mult, ALU.add)
                dve.tensor_scalar(out_s, zcs[:, c, :, 0:TS], cw[:, 0, c:c + 1], cb[:, c:c + 1], ALU.mult, ALU.add)
                for j in range(1, CK):
                    dve.drain()
                    dve.scalar_tensor_tensor(out=out_p, in0=zc[:, c, j:j + T], scalar=cw[:, j, c:c + 1], in1=out_p,
                                             op0=ALU.mult, op1=ALU.add)
                    dve.scalar_tensor_tensor(out=out_s, in0=zcs[:, c, :, j:j + TS], scalar=cw[:, j, c:c + 1], in1=out_s,
                                             op0=ALU.mult, op1=ALU.add)
                dve.drain().then_inc(conv_done, 1)
            for r, (t0, n) in enumerate(REG):
                dve.wait_ge(mean_ps, r + 1)
                m = mixt[:, G:2 * G, t0:t0 + n]
                dve.tensor_tensor(m, m, ps[r][:, 0:n].unsqueeze(1).broadcast_to([P, G, n]), ALU.subtract).then_inc(xc_ready, 1)
            for r, (t0, n) in enumerate(REG):
                dve.wait_ge(lnstd_ready, r + 1)
                dve.reciprocal(rstd_ln[:, t0:t0 + n], rstd_ln[:, t0:t0 + n])
                dve.drain()
                m = mixt[:, G:2 * G, t0:t0 + n]
                dve.tensor_tensor(m, m, rstd_ln[:, t0:t0 + n].unsqueeze(1).broadcast_to([P, G, n]), ALU.mult).then_inc(yn_ready, 1)
            dve.wait_ge(gt1_in, 16 * (1 + NS))
            for i in range(NB + 1):
                n = rows(i)
                dve.wait_ge(mix_ps, i + 1)
                dve.wait_ge(x_in[i % 3], 16 * (3 + i // 3 + 1))
                g = gt1 if i < NB else gt1s
                for h in range(2):
                    dve.tensor_tensor(scr[0:n, h * HALF:(h + 1) * HALF], ps[OB[i % 3][h]][0:n, :], g[0:n, h * HALF:(h + 1) * HALF], ALU.mult)
                dve.drain()
                dve.tensor_tensor(xr[0:n, i % 3], xr[0:n, i % 3], scr[0:n, 0:D], ALU.add).then_inc(x1_ready, 1)
                dve.drain()

        @block.tensor
        def _(pe):
            pe.wait_ge(const_ready, 1)
            pe.wait_ge(csil_ready, 1)
            for k in range(KC):
                last = pe.transpose(ps[0][:, k * NR:(k + 1) * NR], csil[:, k * P:(k + 1) * P], ident[0:NR, 0:NR])
            last.then_inc(ct_ps, 1)
            pe.wait_ge(par_in, 16 * 8)
            pe.transpose(ps[1][:, 0:28], prow[:, :], ident[0:28, 0:28])
            pe.transpose(ps[1][:, P:P + CK * G], cwrow[:, :], ident[0:CK * G, 0:CK * G])
            for g in range(G):
                n = NS * PS
                pe.transpose(ps[2][:, g * n:(g + 1) * n], sprow[:, g * P:(g + 1) * P], ident[0:n, 0:n])
                for h in range(2):
                    last = pe.transpose(ps[3 + h][:, g * n:(g + 1) * n], scrow[:, h, g * P:(g + 1) * P], ident[0:n, 0:n])
            last.then_inc(par_ps, 1)
            pe.wait_ge(ct_ready, 1)
            for n in range(12):
                pe.wait_ge(ada_in[n % 3], 32 * (n // 3 + 1))
                if n >= 3:
                    pe.wait_ge(mod_taken, n - 2)
                bank = ps[5 + n % 3][0:NR, :]
                pe.matmul(bank, ones1[0:1, 0:NR], ada_b[0:1, n % 3], start=True, stop=False)
                for k in range(KC):
                    last = pe.matmul(bank, ct[:, k, :], ada[:, n % 3, k], start=False, stop=(k == KC - 1))
                last.then_inc(mod_ps, 1)
                if n == 3:
                    pe.wait_ge(par_ready, 1)
                if n >= 3:
                    i = n - 3
                    pe.wait_ge(xn_ready, i + 1)
                    if i >= 2:
                        pe.wait_ge(xt_taken, i - 1)
                    for k in range(KC):
                        out = ps[XB[i % 2][k // 4]][:, k % 4 * P:(k % 4 + 1) * P] if i < NB else ps[XB[0][0]][:, k * S:(k + 1) * S]
                        last = pe.transpose(out, xr[0:rows(i), i % 3, k * P:(k + 1) * P], ident[0:rows(i), 0:rows(i)])
                    last.then_inc(xt_ps, 1)
            pe.wait_ge(modrow_ready, 1)
            for a, col in enumerate((SH1, SC1)):
                for k in range(KC):
                    last = pe.transpose(ps[1][:, (a * KC + k) * NR:(a * KC + k + 1) * NR],
                                        modrow[:, col * D + k * P:col * D + (k + 1) * P], ident[0:NR, 0:NR])
            last.then_inc(modt_ps, 1)
            pe.wait_ge(w_in_in, 16 * 3)
            pe.wait_ge(h1_ready, 1)
            for c in range(G):
                for t, n in enumerate((8 + c, 4 + c, c)):
                    m = 3 * c + t
                    if c and t == 0:
                        pe.wait_ge(glu_done, c)
                    if t == 1 and c:
                        pe.wait_ge(act_taken, 2 * c)
                    if t == 2:
                        pe.wait_ge(act_taken, 2 * c + 1)
                    for k in range(KC):
                        for r, (t0, w) in enumerate(REG):
                            last = pe.matmul(ps[3 * (m % 2) + r][:, 0:w], win[:, k, n * P:(n + 1) * P], h1t[:, k, t0:t0 + w],
                                             start=(k == 0), stop=(k == KC - 1))
                    last.then_inc(proj_ps, 1)
            pe.wait_ge(wp_in, 16)
            pe.wait_ge(glu_done, G)
            pe.wait_ge(act_taken, 2 * G)
            for g in range(G):
                pe.wait_ge(diff_ready, g + 1)
                if g >= 2:
                    pe.wait_ge(pool_ready, g - 1)
                for r, (t0, w) in enumerate(REG):
                    last = pe.matmul(ps[3 * (g % 2) + r][:, 0:w], wp[:, g, :], mixt[:, g, t0:t0 + w], start=True, stop=True)
                last.then_inc(pool_ps, 1)
            for s in range(4):
                if s >= 2:
                    pe.wait_ge(st_ready, s - 1)
                if s == 2:
                    pe.wait_ge(new_ready, 1)
                for g in range(G):
                    src = (zp[:, g, T:T + PS], zc[:, g, T:T + CS], new_rows[:, 0, g], new_rows[:, 1, g])[s]
                    n = (PS, CS, S, S)[s]
                    last = pe.transpose(ps[6 + s % 2][0:n, g * P:(g + 1) * P], src, ident[:, :])
                last.then_inc(st_ps, 1)
            pe.wait_ge(conv_done, G)
            pe.wait_ge(pool_ready, G)
            for r, (t0, w) in enumerate(REG):
                for c in range(G):
                    last = pe.matmul(ps[r][:, 0:w], mean_w[:, :], mixt[:, G + c, t0:t0 + w], start=(c == 0), stop=(c == G - 1))
                last.then_inc(mean_ps, 1)
            for r, (t0, w) in enumerate(REG):
                pe.wait_ge(sq_ready, r + 1)
                for c in range(G):
                    last = pe.matmul(ps[3 + r][:, 0:w], mean_w[:, :], sq[:, c, t0:t0 + w], start=(c == 0), stop=(c == G - 1))
                last.then_inc(var_ps, 1)
            pe.wait_ge(w_out_in, 16)
            pe.wait_ge(bout_in, 16)
            pe.wait_ge(st_ready, 4)
            pe.wait_ge(lnstd_ready, 1)
            for i in range(NB + 1):
                n = rows(i)
                if i >= 3:
                    pe.wait_ge(x1_ready, i - 2)
                if i in (0, 4, 8):
                    pe.wait_ge(cm_ready, i // 4 + 1)
                for h in range(2):
                    bank = ps[OB[i % 3][h]][0:n, :]
                    pe.matmul(bank, ones1[0:1, 0:n], bout[:, h * HALF:(h + 1) * HALF], start=True, stop=False)
                    for k in range(KC):
                        last = pe.matmul(bank, mixt[:, k, i * P:i * P + n], wout[:, k, h * HALF:(h + 1) * HALF],
                                         start=False, stop=(k == KC - 1))
                last.then_inc(mix_ps, 1)


def expert_phase(nc, ps, ident, eps_c, wq, wq_in, x1_dram, mod_dram, sub_keys, u_table, v_table, g_final,
                 y_prompt, y_sample):
    with ExitStack() as ctx:
        def sb(name, shape, dt=F32):
            return ctx.enter_context(nc.sbuf_tensor(name, shape, dt))

        def sem(name):
            return ctx.enter_context(nc.semaphore(name))

        keyt = sb("keyt", [P, 2 * H, NKEY])
        u_ring = sb("u_ring", [P, RING, D])
        v_ring = sb("v_ring", [P, RING, D])
        krow = v_ring[:, 0:2, :].rearrange("p a (b k) -> p (a b) k", k=P)
        mod2 = sb("mod2", [P, 3, D])
        gfin = sb("gfin", [P, D])
        x1 = sb("x1", [P, D])
        h2n = sb("h2n", [P, D])
        h2c = sb("h2c", [P, D])
        y = sb("y", [P, D])
        scratch = sb("scratch", [P, D])
        h2t = sb("h2t", [P, KC, P])
        qt = sb("qt", [P, 4, P])
        s_sb = sb("s_sb", [P, 4, NKEY])
        s_rep = sb("s_rep", [P, NKEY])
        sv = sb("sv", [P, 4, K])
        si = sb("si", [P, 4, K], U32)
        sif = sb("sif", [P, 4, K])
        comb = sb("comb", [P, K * K])
        comb_rep = sb("comb_rep", [P, K * K])
        fpos = sb("fpos", [P, 2, K], U32)
        fhalf = sb("fhalf", [P, 2, 2 * K], U32)
        fhalff = sb("fhalff", [P, 2, 2 * K])
        hot = sb("hot", [P, 2, K, K])
        keyno = sb("keyno", [P, 2, 2, K])
        iota = sb("iota", [P, K])
        fv = sb("fv", [P, H, K])
        fsum = sb("fsum", [P, H])
        gaten = sb("gaten", [P, H, K])
        gatec = sb("gatec", [P, H, K])
        eidn = sb("eidn", [P, H * K], U32)
        eidc = sb("eidc", [P, H * K], U32)
        eids = sb("eids", [P, PK], U32)
        none = sb("none", [P, H * K], U32)
        mark = sb("mark", [1, 1])
        sel = sb("sel", [P, P])
        dot = sb("dot", [P, K])
        gel = sb("gel", [P, K])
        act_w = sb("act_w", [P, K])
        diag = sb("diag", [P, RING, P])
        zeros = sb("zeros", [1, HALF], BF16)
        st = sb("st", [P, 6])

        key_in, mod2_in, gfin_in, x1_in, y_in = (sem(n) for n in ("key_in", "mod2_in", "gfin_in", "x1_in", "y_in"))
        u_in = [sem(f"u_in{i}") for i in range(RING)]
        v_in = [sem(f"v_in{i}") for i in range(RING)]
        u_free, v_free, dot_free, diag_ready = (
            sem(n) for n in ("u_free", "v_free", "dot_free", "diag_ready"))
        const2, key_ps, key_ready = sem("const2"), sem("key_ps"), sem("key_ready")
        ss_done, std_done, h2_ready, h2_ps, h2t_ready = (sem(n) for n in ("ss_done", "std_done", "h2_ready", "h2_ps", "h2t_ready"))
        q_ps, qt_ready, s_ps, s_taken = sem("q_ps"), sem("qt_ready"), sem("s_ps"), sem("s_taken")
        turns, fold_ready = sem("turns"), sem("fold_ready")
        top_ready, exp_ready, found, eid_taken, gate_taken = (
            sem(n) for n in ("top_ready", "exp_ready", "found", "eid_taken", "gate_taken"))
        acc_ready, acc_free, fin_ss, fin_std, y_ready, y_stored = (
            sem(n) for n in ("acc_ready", "acc_free", "fin_ss", "fin_std", "y_ready", "y_stored"))

        u_rows, v_rows = u_table[0], v_table[0]
        acc = ps[0:2]
        S2, A2, GT = range(3)
        LAST = NB - 1
        NCH = H * CPH
        NCP = NCH // PARTS

        steady = {"norm": {0: 1}, "query": {}, "piece": {}, "soft": {}}
        for part in range(PARTS):
            steady["query"][1 + 6 * part] = [(1, part)]
            for i in range(PIECES):
                steady["piece"][3 + 6 * part + i] = [(1, part, i)]
            steady["soft"][3 + 6 * part + PIECES - 2] = [(1, part)]
        steps = [(0, part, i) for part in range(1, PARTS) for i in range(PIECES)] + ["norm", "gap", "gap"]
        steps += [(1, part, i) for part in range(PARTS) for i in range(PIECES)]
        first = {"norm": {}, "query": {}, "piece": {}, "soft": {}}
        for n, step in enumerate(steps):
            c = n * (NCH - 1) // len(steps)
            if step == "norm":
                first["norm"][c] = 1
                first["query"].setdefault(c + 1, []).append((1, 0))
            elif step != "gap":
                df, part, i = step
                first["piece"].setdefault(c, []).append(step)
                if i == 0 and (df, part) not in ((0, PARTS - 1), (1, PARTS - 1)):
                    first["query"].setdefault(c + 1, []).append((df, part + 1))
                if i == PIECES - 2:
                    first["soft"].setdefault(c, []).append((df, part))
        none_beside = {"norm": {}, "query": {}, "piece": {}, "soft": {}}

        block = ctx.enter_context(nc.Block())


        @block.sync
        def _(sp):
            sp.dma_start(x1[:, :], x1_dram[0:P, :]).then_inc(x1_in, 16)
            for a, col in enumerate((SH2, SC2, GT2)):
                sp.dma_start(mod2[:, a], mod_dram[0:1, col * D:(col + 1) * D].broadcast_to([P, D])).then_inc(mod2_in, 16)
            sp.dma_start(krow, sub_keys[0].rearrange("h p m k -> m (h p) k")).then_inc(key_in, 16)
            sp.dma_start(gfin[:, :], g_final.rearrange("(a d) -> a d", a=1).broadcast_to([P, D])).then_inc(gfin_in, 16)
            sp.dma_start(y[:, :], x1_dram[0:P, :]).then_inc(y_in, 16)

            def x1_load(f):
                sp.wait_ge(h2_ready, f)
                sp.dma_start(x1[:, :], x1_dram[bass.ds(f * P, P), :]).then_inc(x1_in, 16)

            def store(b):
                sp.wait_ge(y_ready, b + 1)
                sp.dma_start(y_prompt[0, bass.ds(b * P, P), :], y[:, :]).then_inc(y_stored, 16)
                sp.wait_ge(y_stored, (b + 1) * 16)

            def y_load(b):
                sp.dma_start(y[:, :], x1_dram[bass.ds(b * P, P), :]).then_inc(y_in, 16)

            x1_load(1)
            x1_load(2)
            with sp.Fori(1, LAST - 1) as b:
                store(b - 1)
                y_load(b)
                x1_load(b + 2)
            store(LAST - 2)
            y_load(LAST - 1)
            sp.wait_ge(h2_ready, LAST + 1)
            for q in range(4):
                sp.dma_start(x1[q * S:(q + 1) * S, :], x1_dram[T:NT, :]).then_inc(x1_in, 16)
                for r in range(NS):
                    p0 = q * S + r * TS
                    for a, col in enumerate((SH2, SC2)):
                        sp.dma_start(mod2[p0:p0 + TS, a], mod_dram[1 + r:2 + r, col * D:(col + 1) * D].broadcast_to([TS, D])).then_inc(mod2_in, 16)
            store(LAST - 1)
            y_load(LAST)
            store(LAST)
            for q in range(4):
                sp.dma_start(y[q * S:(q + 1) * S, :], x1_dram[T:NT, :]).then_inc(y_in, 16)
                for r in range(NS):
                    p0 = q * S + r * TS
                    sp.dma_start(mod2[p0:p0 + TS, GT], mod_dram[1 + r:2 + r, GT2 * D:(GT2 + 1) * D].broadcast_to([TS, D])).then_inc(mod2_in, 16)
            sp.wait_ge(y_ready, NB + 1)
            sp.dma_start(y_sample.rearrange("b t d -> (b t) d"), y[0:S, :]).then_inc(y_stored, 16)
            sp.wait_ge(y_stored, (NB + 1) * 16)

        @block.gpsimd
        def _(pool):
            pool.memset(sel[:, :], 0.0)
            pool.memset(zeros[:, :], 0.0)
            pool.memset(none[:, :], 0)
            for k in range(K):
                pool.memset(iota[:, k:k + 1], float(k))
            for q in range(-3, 4):
                pool.drain()
                pool.affine_select(out=sel[:, :], in_=sel[:, :], compare_op=ALU.not_equal, fill=1.0, base=q * S,
                                   pattern=[[-1, P]], channel_multiplier=1)
            pool.drain().then_inc(const2, 1)
            pool.drain().then_inc(turns, 1)

            def turn(n, ready, count):
                pool.wait_ge(turns, n + 1)
                pool.wait_ge(ready, count)
                pool.tensor_tensor(mark[:, :], iota[0:1, 0:1], iota[0:1, 1:2], ALU.add).then_inc(turns, 1)

            def chunk(n, c, eid=eidc):
                for a, (ring, landed, free, table) in enumerate(((u_ring, u_in, u_free, u_rows), (v_ring, v_in, v_free, v_rows))):
                    turn(2 * n + a, free, n + 1)
                    for j in range(CH):
                        slot = c % 2 * CH + j
                        pool.indirect_dma_start(ring[:, slot], None, table,
                                                bass.IndirectOffsetOnAxis(ap=eid[:, c * CH + j:c * CH + j + 1], axis=0)
                                                ).then_inc(landed[slot], 16)

            def gathers(b):
                for c in range(NCH):
                    if c % NCP == 0:
                        part = c // NCP
                        cols = slice(part * PK, (part + 1) * PK)
                        pool.wait_ge(turns, 2 * (b * NCH + c) + 1)
                        pool.wait_ge(found, b * PARTS + part + 1)
                        pool.tensor_tensor(eidc[:, cols], eidn[:, cols], none[:, cols], ALU.add).then_inc(eid_taken, 1)
                        pool.wait_ge(eid_taken, b * PARTS + part + 1)
                    chunk(b * NCH + c, c)

            gathers(0)
            with pool.Fori(1, LAST) as b:
                gathers(b)
            gathers(LAST)
            pool.wait_ge(fold_ready, 1)
            for c in range(NCP):
                chunk(NB * NCH + c, c, eids)

        @block.scalar
        def _(act):
            gate = gatec[:, :, :].rearrange("p h k -> p (h k)")
            act.wait_ge(key_ps, 1)
            for i in range(4):
                last = act.activation(keyt[:, 4 * i:4 * i + 4, :], ps[2 + i][:, :].rearrange("p (a m) -> p a m", a=4), ACT.Copy)
            last.then_inc(key_ready, 1)

            def root(f, col, ready, done):
                act.wait_ge(ready, f + 1)
                act.activation(st[:, col + 1:col + 2], st[:, col:col + 1], ACT.Sqrt, bias=eps_c[:, :], scale=1.0 / D).then_inc(done, 1)

            def query(f, part):
                if part == 0:
                    act.wait_ge(h2_ps, f + 1)
                    for i in range(2):
                        last = act.activation(h2t[:, 4 * i:4 * i + 4, :], ps[2 + i][:, :].rearrange("p (a t) -> p a t", a=4), ACT.Copy)
                    last.then_inc(h2t_ready, 1)
                act.wait_ge(q_ps, f * PARTS + part + 1)
                act.activation(qt[:, :, :], ps[4][:, :].rearrange("p (a t) -> p a t", a=4), ACT.Copy).then_inc(qt_ready, 1)

            def softmax(f, part):
                act.wait_ge(top_ready, f * PARTS + part + 1)
                g = gaten[:, 2 * part:2 * part + 2, :]
                act.activation(g, g, ACT.Exp).then_inc(exp_ready, 1)

            def chunk(n, c, fold):
                c0 = c % CPH * CH
                act.wait_ge(u_free, n + 3)
                act.activation(gel[:, c0:c0 + CH], dot[:, c0:c0 + CH], ACT.Gelu).then_inc(dot_free, 1)
                act.drain()
                for j in range(CH):
                    act.activation(act_w[:, c0 + j:c0 + j + 1], gel[:, c0 + j:c0 + j + 1], ACT.Copy,
                                   scale=gate[:, c * CH + j:c * CH + j + 1])
                act.drain()
                act.wait_ge(v_free, n + 1)
                for j in range(CH):
                    last = act.activation(diag[:, c % 2 * CH + j, :], fold[:, :], ACT.Copy, scale=act_w[:, c0 + j:c0 + j + 1])
                last.then_inc(diag_ready, 1)

            def block_steps(b, beside, chunks, is_first=False):
                for c in range(chunks):
                    if c % NCP == 0:
                        part = c // NCP
                        if chunks == NCH:
                            act.wait_ge(found, b * PARTS + part + 1)
                            act.activation(gatec[:, 2 * part:2 * part + 2, :], gaten[:, 2 * part:2 * part + 2, :], ACT.Copy)
                        else:
                            act.wait_ge(found, (b + 1) * PARTS)
                            for q in range(4):
                                act.activation(gatec[q * S:(q + 1) * S, 0:2, :], gaten[q * S:(q + 1) * S, 2 * q:2 * q + 2, :], ACT.Copy)
                        act.drain().then_inc(gate_taken, 1)
                    chunk(b * NCH + c, c, ident if chunks == NCH else sel)
                    if c == 0 and not is_first:
                        root(b - 1, 3, fin_ss, fin_std)
                    if c in beside["norm"]:
                        root(b + 1, 0, ss_done, std_done)
                    for df, part in beside["query"].get(c, []):
                        query(b + df, part)
                    for df, part in beside["soft"].get(c, []):
                        softmax(b + df, part)

            root(0, 0, ss_done, std_done)
            query(0, 0)
            query(0, 1)
            softmax(0, 0)
            block_steps(0, first, NCH, True)
            with act.Fori(1, LAST) as b:
                block_steps(b, steady, NCH)
            block_steps(LAST, steady, NCH)
            act.wait_ge(const2, 1)
            block_steps(NB, none_beside, NCP)
            root(NB, 3, fin_ss, fin_std)

        @block.vector
        def _(dve):
            dve.drain().then_inc(u_free, 2)
            dve.drain().then_inc(v_free, 2)
            dve.drain().then_inc(dot_free, CPH)
            dve.drain().then_inc(acc_free, 1)
            dve.wait_ge(const2, 1)

            def norm(f, loads):
                dve.wait_ge(x1_in, 16 * loads)
                dve.tensor_tensor_reduce(scratch[:, :], x1[:, :], x1[:, :], 1.0, 0.0, ALU.mult, ALU.add, st[:, 0:1]).then_inc(ss_done, 1)
                dve.wait_ge(std_done, f + 1)
                dve.reciprocal(st[:, 2:3], st[:, 1:2])
                dve.drain()
                dve.scalar_tensor_tensor(out=h2n[:, :], in0=x1[:, :], scalar=st[:, 2:3], in1=mod2[:, A2], op0=ALU.mult, op1=ALU.mult)
                dve.drain()
                dve.tensor_tensor(h2n[:, :], h2n[:, :], mod2[:, S2], ALU.add).then_inc(h2_ready, 1)

            def top16(vals, idx, src, rep):
                dve.max(vals[:, 0:8], src)
                dve.drain()
                dve.match_replace(rep, vals[:, 0:8], src, -3.0e38)
                dve.max_index(idx[:, 0:8], vals[:, 0:8], src)
                dve.drain()
                dve.max(vals[:, 8:16], rep)
                dve.drain()
                dve.max_index(idx[:, 8:16], vals[:, 8:16], rep)
                dve.drain()

            def key_top(i):
                top16(sv[:, i], si[:, i], s_sb[:, i], s_rep[:, :])

            def pair_top(part, j):
                dve.tensor_tensor(comb[:, :].rearrange("p (a b) -> p a b", a=K), sv[:, 2 * j].unsqueeze(2).broadcast_to([P, K, K]),
                                  sv[:, 2 * j + 1].unsqueeze(1).broadcast_to([P, K, K]), ALU.add)
                dve.drain()
                top16(fv[:, 2 * part + j], fpos[:, j], comb[:, :], comb_rep[:, :])

            def key_numbers(a):
                shape = [P, 2, K, K]
                dve.tensor_tensor(hot[:, :, :, :], fhalff[:, :, a * K:(a + 1) * K].unsqueeze(3).broadcast_to(shape),
                                  iota[:, :].unsqueeze(1).unsqueeze(1).broadcast_to(shape), ALU.is_equal)
                dve.drain()
                dve.tensor_tensor(hot[:, :, :, :], hot[:, :, :, :], sif[:, a:4:2, :].unsqueeze(2).broadcast_to(shape), ALU.mult)
                dve.drain()
                dve.tensor_reduce(keyno[:, a], hot[:, :, :, :], AX, ALU.add)
                dve.drain()

            def piece(f, part, i, own=False):
                g = gaten[:, 2 * part:2 * part + 2, :]
                if i == 0:
                    dve.wait_ge(s_ps, f * PARTS + part + 1)
                    dve.tensor_copy(s_sb[:, :, :], ps[5][:, :].rearrange("p (a m) -> p a m", a=4)).then_inc(s_taken, 1)
                    dve.drain()
                    key_top(0)
                elif i == 1:
                    key_top(1)
                    key_top(2)
                elif i == 2:
                    key_top(3)
                    dve.tensor_copy(sif[:, :, :], si[:, :, :])
                    pair_top(part, 0)
                elif i == 3:
                    pair_top(part, 1)
                    dve.tensor_scalar(fhalf[:, :, 0:K], fpos[:, :, :], 4, None, ALU.logical_shift_right)
                    dve.tensor_scalar(fhalf[:, :, K:2 * K], fpos[:, :, :], K - 1, None, ALU.bitwise_and)
                    dve.drain()
                    dve.tensor_copy(fhalff[:, :, :], fhalf[:, :, :])
                elif i == 4:
                    if not own:
                        dve.wait_ge(gate_taken, (f - 1) * PARTS + part + 1)
                    fvp = fv[:, 2 * part:2 * part + 2, :]
                    dve.tensor_tensor(g, fvp, fvp[:, :, 0:1].broadcast_to([P, 2, K]), ALU.subtract)
                    dve.drain().then_inc(top_ready, 1)
                    key_numbers(0)
                else:
                    key_numbers(1)
                    if not own:
                        dve.wait_ge(eid_taken, (f - 1) * PARTS + part + 1)
                    dve.scalar_tensor_tensor(out=eidn[:, part * PK:(part + 1) * PK].rearrange("p (a k) -> p a k", a=2),
                                             in0=keyno[:, 0], scalar=float(NKEY), in1=keyno[:, 1], op0=ALU.mult, op1=ALU.add)
                    dve.wait_ge(exp_ready, f * PARTS + part + 1)
                    dve.tensor_reduce(fsum[:, 0:2], g, AX, ALU.add)
                    dve.drain()
                    dve.reciprocal(fsum[:, 0:2], fsum[:, 0:2])
                    dve.drain()
                    dve.tensor_tensor(g, g, fsum[:, 0:2].unsqueeze(2).broadcast_to([P, 2, K]), ALU.mult)
                    dve.drain().then_inc(found, 1)

            def chunk(n, c, r):
                c0 = c % CPH * CH
                dve.wait_ge(dot_free, n + 1)
                for j in range(CH):
                    slot = c % 2 * CH + j
                    dve.wait_ge(u_in[slot], 16 * (r + 1))
                    last = dve.tensor_tensor_reduce(u_ring[:, slot], u_ring[:, slot], h2c[:, :], 1.0, 0.0, ALU.mult, ALU.add,
                                                    dot[:, c0 + j:c0 + j + 1])
                last.then_inc(u_free, 1)
                dve.drain()

            def finish(b, loads, mods):
                dve.wait_ge(acc_ready, b + 1)
                dve.wait_ge(mod2_in, 16 * mods)
                for i in range(2):
                    dve.tensor_tensor(scratch[:, i * HALF:(i + 1) * HALF], acc[i][:, :], mod2[:, GT, i * HALF:(i + 1) * HALF], ALU.mult)
                dve.drain().then_inc(acc_free, 1)
                dve.wait_ge(y_in, 16 * loads)
                dve.tensor_tensor(y[:, :], y[:, :], scratch[:, :], ALU.add)
                dve.drain()
                dve.tensor_tensor_reduce(scratch[:, :], y[:, :], y[:, :], 1.0, 0.0, ALU.mult, ALU.add, st[:, 3:4]).then_inc(fin_ss, 1)
                dve.wait_ge(fin_std, b + 1)
                dve.reciprocal(st[:, 5:6], st[:, 4:5])
                dve.drain()
                dve.scalar_tensor_tensor(out=y[:, :], in0=y[:, :], scalar=st[:, 5:6], in1=gfin[:, :], op0=ALU.mult, op1=ALU.mult).then_inc(y_ready, 1)
                dve.drain()

            def block_steps(b, beside, chunks, is_first=False, loads=None):
                dve.drain()
                dve.tensor_copy(h2c[:, :], h2n[:, :])
                dve.drain()
                for c in range(chunks):
                    chunk(b * NCH + c, c, b * (NCH // 2) + c // 2)
                    if c == 0 and not is_first:
                        finish(b - 1, b, 3)
                    if c in beside["norm"]:
                        norm(b + 1, loads or b + 2)
                        dve.drain()
                    for df, part, i in beside["piece"].get(c, []):
                        piece(b + df, part, i, own=is_first and df == 0)
                    if loads and c == 3 + 6 * PARTS:
                        for q in range(4):
                            dve.tensor_copy(eids[q * S:(q + 1) * S, :], eidn[q * S:(q + 1) * S, q * PK:(q + 1) * PK])
                        dve.drain().then_inc(fold_ready, 1)

            dve.wait_ge(mod2_in, 16 * 3)
            norm(0, 1)
            for i in range(PIECES):
                piece(0, 0, i, own=True)
            dve.wait_ge(gfin_in, 16)
            block_steps(0, first, NCH, True)
            with dve.Fori(1, LAST) as b:
                block_steps(b, steady, NCH)
            dve.wait_ge(mod2_in, 16 * (3 + 4 * NS * 2))
            block_steps(LAST, steady, NCH, loads=NB + 4)
            block_steps(NB, none_beside, NCP)
            finish(NB, NB + 4, 3 + 4 * NS * 3)

        @block.tensor
        def _(pe):
            pe.wait_ge(key_in, 16)
            for i in range(2 * H):
                last = pe.transpose(ps[2 + i // 4][:, i % 4 * P:(i % 4 + 1) * P], krow[:, i, :], ident[:, :])
            last.then_inc(key_ps, 1)
            pe.wait_ge(key_ready, 1)

            def query(f, part, own=False):
                if part == 0:
                    pe.wait_ge(h2_ready, f + 1)
                    for k in range(KC):
                        last = pe.transpose(ps[2 + k // 4][:, k % 4 * P:(k % 4 + 1) * P], h2n[:, k * P:(k + 1) * P], ident[:, :])
                    last.then_inc(h2_ps, 1)
                    pe.wait_ge(h2t_ready, f + 1)
                if own:
                    pe.wait_ge(wq_in[part], 16)
                for i in range(4):
                    for k in range(KC):
                        last = pe.matmul(ps[4][:, i * P:(i + 1) * P], wq[:, part, k, i * P:(i + 1) * P], h2t[:, k, :],
                                         start=(k == 0), stop=(k == KC - 1))
                last.then_inc(q_ps, 1)
                pe.wait_ge(qt_ready, f * PARTS + part + 1)
                pe.wait_ge(s_taken, f * PARTS + part)
                for i in range(4):
                    last = pe.matmul(ps[5][:, i * P:(i + 1) * P], qt[:, i, :], keyt[:, part * 4 + i, :], start=True, stop=True)
                last.then_inc(s_ps, 1)

            def zero(start):
                for i in range(2):
                    last = pe.matmul(acc[i][:, :], zeros[0:1, 0:P], zeros[0:1, :], start=start, stop=not start, skip_group_check=True)
                return last

            def chunk(n, c, r):
                pe.wait_ge(diag_ready, n + 1)
                for j in range(CH):
                    slot = c % 2 * CH + j
                    pe.wait_ge(v_in[slot], 16 * (r + 1))
                    for i in range(2):
                        last = pe.matmul(acc[i][:, :], diag[:, slot, :], v_ring[:, slot, i * HALF:(i + 1) * HALF],
                                         start=False, stop=False, skip_group_check=True)
                last.then_inc(v_free, 1)

            def block_steps(b, beside, chunks, is_first=False):
                pe.wait_ge(acc_free, b + 1)
                zero(True)
                for c in range(chunks):
                    chunk(b * NCH + c, c, b * (NCH // 2) + c // 2)
                    for df, part in beside["query"].get(c, []):
                        query(b + df, part, own=is_first and df == 0)
                zero(False).then_inc(acc_ready, 1)

            pe.wait_ge(const2, 1)
            query(0, 0, own=True)
            query(0, 1, own=True)
            block_steps(0, first, NCH, True)
            with pe.Fori(1, LAST) as b:
                block_steps(b, steady, NCH)
            block_steps(LAST, steady, NCH)
            block_steps(NB, none_beside, NCP)


_INS = ['x_prompt', 'x_sample', 'state_pool', 'state_conv', 'c_prompt', 'c_sample', 'w_ada', 'b_ada', 'g_norm1', 'g_norm2',
        'w_in', 'b_in', 'w_pool', 'pool_scale', 'conv_w', 'conv_b', 'ln_g', 'ln_b', 'w_out', 'b_out', 'w_query', 'sub_keys',
        'u_table', 'v_table', 'g_final']
_OUTS = [(1, T, D), (NS, TS, D), (1, 1, PS, GW), (1, 1, CS, GW), (1, NS, PS, GW), (1, NS, CS, GW)]


def kernel(**inputs):
    import numpy as _np
    import concourse.bacc as _bacc
    from concourse import mybir as _mybir
    from concourse.bass_utils import run_bass_kernel_spmd as _run

    nc = _bacc.Bacc("TRN2", target_bir_lowering=False, num_devices=1)
    arrays, args = {}, []
    for name in _INS:
        a = _np.ascontiguousarray(inputs[name])
        arrays[f"in_{name}_dram"] = a
        args.append(nc.dram_tensor(f"in_{name}_dram", a.shape, _mybir.dt.from_np(a.dtype), kind="ExternalInput").ap())
    for i, shape in enumerate(_OUTS):
        args.append(nc.dram_tensor(f"out_{i}_dram", shape, _mybir.dt.float32, kind="ExternalOutput").ap())
    build(nc, *args)
    r = _run(nc, [arrays], core_ids=[0])
    return tuple(r.results[0][f"out_{i}_dram"] for i in range(len(_OUTS)))
```
